# Optimizing a Trainium2 kernel written in Bass

```python
import math
import jax, jax.numpy as jnp
from jax import lax
import numpy as np

D_MODEL = 1024
BATCH = 1
SEQ = 512
DEPTH = 2

N_MIXERS = 2
N_RET_LAYERS = (DEPTH + N_MIXERS - 1) // N_MIXERS
N_S5_LAYERS = DEPTH // N_MIXERS
N_MOD = 9
D_FF = 2816
RET_HEADS = 4
RET_QK_DIM = D_MODEL // RET_HEADS
RET_V_DIM = 2 * D_MODEL // RET_HEADS
RET_CHUNK = 128
ROPE_THETA = 10000.0
S5_GROUP = 16
S5_GROUPS = D_MODEL // S5_GROUP
S5_STATE = 64
DT_MIN = 0.001
DT_MAX = 0.1
NORM_EPS = 1e-6
GN_EPS = 1e-5

kernel_name = "hybrid_retention_s5_macaron_adaln"

def rms_norm(x, g):
    xf = x.astype(jnp.float32)
    y = xf * lax.rsqrt(jnp.mean(xf * xf, axis=-1, keepdims=True) + NORM_EPS)
    return (y * g.astype(jnp.float32)).astype(x.dtype)

def modulate(h, shift, scale):
    return h * (1.0 + scale[:, None, :]) + shift[:, None, :]

def swiglu_ffn(h, w_in, w_out):
    gate, up = jnp.split(h @ w_in, 2, axis=-1)
    return (jax.nn.silu(gate) * up) @ w_out

def rotary(t, positions):
    half = t.shape[-1] // 2
    inv_freq = ROPE_THETA ** (-jnp.arange(half, dtype=jnp.float32) / half)
    ang = positions.astype(jnp.float32)[..., None] * inv_freq
    cos = jnp.cos(ang)[:, :, None, :]
    sin = jnp.sin(ang)[:, :, None, :]
    t1, t2 = t[..., :half], t[..., half:]
    return jnp.concatenate([t1 * cos - t2 * sin, t1 * sin + t2 * cos], axis=-1)

def retention(h, positions, w_in, w_out):
    B, L, _ = h.shape
    H, dk, dv, C = RET_HEADS, RET_QK_DIM, RET_V_DIM, RET_CHUNK
    N = L // C
    qk_w, v_w = H * dk, H * dv
    q, k, v, g = jnp.split(h @ w_in, [qk_w, 2 * qk_w, 2 * qk_w + v_w], axis=-1)
    q = rotary(q.reshape(B, L, H, dk).astype(jnp.float32), positions)
    k = rotary(k.reshape(B, L, H, dk).astype(jnp.float32), positions) * (dk ** -0.5)
    v = v.reshape(B, L, H, dv).astype(jnp.float32)

    log_gamma = jnp.log(1.0 - jnp.power(2.0, -5.0 - jnp.arange(H, dtype=jnp.float32)))
    pos = jnp.arange(C, dtype=jnp.float32)
    diff = pos[:, None] - pos[None, :]
    decay_mask = jnp.where(diff >= 0,
                           jnp.exp(log_gamma[:, None, None] * jnp.maximum(diff, 0.0)),
                           0.0)
    q_decay = jnp.exp(log_gamma[:, None] * (pos + 1.0))[None, :, :, None]
    k_decay = jnp.exp(log_gamma[:, None] * (C - 1.0 - pos))[None, :, :, None]
    chunk_decay = jnp.exp(log_gamma * C)[None, :, None, None]

    def to_chunks(t):
        return t.reshape(B, N, C, H, -1).transpose(1, 0, 3, 2, 4)

    def step(state, qkv):
        qc, kc, vc = qkv
        scores = jnp.einsum('bhid,bhjd->bhij', qc, kc) * decay_mask
        inner = jnp.einsum('bhij,bhje->bhie', scores, vc)
        cross = jnp.einsum('bhid,bhde->bhie', qc, state) * q_decay
        state = state * chunk_decay + jnp.einsum('bhjd,bhje->bhde', kc * k_decay, vc)
        return state, inner + cross

    state0 = jnp.zeros((B, H, dk, dv), jnp.float32)
    _, o = lax.scan(step, state0, (to_chunks(q), to_chunks(k), to_chunks(v)))
    o = o.transpose(1, 0, 3, 2, 4).reshape(B, L, H, dv)
    mu = jnp.mean(o, axis=-1, keepdims=True)
    var = jnp.mean(jnp.square(o - mu), axis=-1, keepdims=True)
    o = ((o - mu) * lax.rsqrt(var + GN_EPS)).reshape(B, L, v_w).astype(h.dtype)
    return (jax.nn.silu(g) * o) @ w_out

def s5_layer(u, a_re, a_im, b_re, b_im, c_re, c_im, d_skip, log_dt, w_glu):
    Bsz, L, Dm = u.shape
    G, P, K = S5_GROUPS, S5_STATE, S5_GROUP
    f32 = jnp.float32
    A = lax.complex(a_re.astype(f32), a_im.astype(f32))
    dt = jnp.exp(log_dt.astype(f32))[:, None]
    A_bar = jnp.exp(dt * A)
    B_mat = lax.complex(b_re.astype(f32), b_im.astype(f32))
    B_bar = ((A_bar - 1.0) / A)[..., None] * B_mat
    C_mat = lax.complex(c_re.astype(f32), c_im.astype(f32))

    uf = u.astype(f32)
    ug = uf.reshape(Bsz, L, G, K).astype(jnp.complex64)
    bu = jnp.einsum('blgk,gpk->blgp', ug, B_bar)
    a = jnp.broadcast_to(A_bar, (1, L, G, P))

    def combine(left, right):
        a_l, b_l = left
        a_r, b_r = right
        return a_l * a_r, a_r * b_l + b_r

    _, states = lax.associative_scan(combine, (a, bu), axis=1)
    y = jnp.einsum('gkp,blgp->blgk', C_mat, states).real.reshape(Bsz, L, Dm)
    y = jax.nn.gelu(y + d_skip.astype(f32) * uf).astype(u.dtype)
    y1, y2 = jnp.split(y @ w_glu, 2, axis=-1)
    return y1 * jax.nn.sigmoid(y2)

def setup_inputs(seed: int = 0) -> dict:
    key = jax.random.key(seed)
    ks = jax.random.split(key, 20)
    D, f32 = D_MODEL, jnp.float32
    G, P, K = S5_GROUPS, S5_STATE, S5_GROUP
    nrm = lambda k, shape, s: jax.random.normal(k, shape, f32) * s
    x = nrm(ks[0], (BATCH, SEQ, D), 1.0)
    c = nrm(ks[1], (BATCH, D), 1.0)
    positions = jnp.broadcast_to(jnp.arange(SEQ, dtype=jnp.int32), (BATCH, SEQ))
    ada_w = nrm(ks[2], (DEPTH, D, N_MOD * D), 0.5 * D ** -0.5)
    ada_b = nrm(ks[3], (DEPTH, N_MOD * D), 0.01)
    norm_g = 1.0 + nrm(ks[4], (DEPTH, 3, D), 0.02)
    ffn_w_in = nrm(ks[5], (DEPTH, 2, D, 2 * D_FF), D ** -0.5)
    ffn_w_out = nrm(ks[6], (DEPTH, 2, D_FF, D), D_FF ** -0.5)
    ret_in_w = 2 * RET_HEADS * RET_QK_DIM + 2 * RET_HEADS * RET_V_DIM
    ret_w_in = nrm(ks[7], (N_RET_LAYERS, D, ret_in_w), D ** -0.5)
    ret_w_out = nrm(ks[8], (N_RET_LAYERS, RET_HEADS * RET_V_DIM, D), (RET_HEADS * RET_V_DIM) ** -0.5)
    s5_a_re = -0.5 + nrm(ks[9], (N_S5_LAYERS, G, P), 0.01)
    s5_a_im = jnp.broadcast_to(math.pi * jnp.arange(P, dtype=f32), (N_S5_LAYERS, G, P))
    s5_b_re = nrm(ks[10], (N_S5_LAYERS, G, P, K), (2 * K) ** -0.5)
    s5_b_im = nrm(ks[11], (N_S5_LAYERS, G, P, K), (2 * K) ** -0.5)
    s5_c_re = nrm(ks[12], (N_S5_LAYERS, G, K, P), (2 * P) ** -0.5)
    s5_c_im = nrm(ks[13], (N_S5_LAYERS, G, K, P), (2 * P) ** -0.5)
    s5_d = nrm(ks[14], (N_S5_LAYERS, D), 1.0)
    s5_log_dt = jax.random.uniform(ks[15], (N_S5_LAYERS, G), f32,
                                   math.log(DT_MIN), math.log(DT_MAX))
    s5_w_glu = nrm(ks[16], (N_S5_LAYERS, D, 2 * D), D ** -0.5)
    final_g = 1.0 + nrm(ks[17], (D,), 0.02)
    return {"x": x, "c": c, "positions": positions,
            "ada_w": ada_w, "ada_b": ada_b, "norm_g": norm_g,
            "ffn_w_in": ffn_w_in, "ffn_w_out": ffn_w_out,
            "ret_w_in": ret_w_in, "ret_w_out": ret_w_out,
            "s5_a_re": s5_a_re, "s5_a_im": s5_a_im,
            "s5_b_re": s5_b_re, "s5_b_im": s5_b_im,
            "s5_c_re": s5_c_re, "s5_c_im": s5_c_im,
            "s5_d": s5_d, "s5_log_dt": s5_log_dt, "s5_w_glu": s5_w_glu,
            "final_g": final_g}

def reference(x, c, positions, ada_w, ada_b, norm_g, ffn_w_in, ffn_w_out,
              ret_w_in, ret_w_out, s5_a_re, s5_a_im, s5_b_re, s5_b_im,
              s5_c_re, s5_c_im, s5_d, s5_log_dt, s5_w_glu, final_g):
    c_act = jax.nn.silu(c)
    for i in range(DEPTH):
        mods = jnp.split(c_act @ ada_w[i] + ada_b[i], N_MOD, axis=-1)
        sh1, sc1, g1, sh2, sc2, g2, sh3, sc3, g3 = mods
        h = modulate(rms_norm(x, norm_g[i, 0]), sh1, sc1)
        x = x + 0.5 * g1[:, None, :] * swiglu_ffn(h, ffn_w_in[i, 0], ffn_w_out[i, 0])
        h = modulate(rms_norm(x, norm_g[i, 1]), sh2, sc2)
        j = i // N_MIXERS
        if i % N_MIXERS == 0:
            m = retention(h, positions, ret_w_in[j], ret_w_out[j])
        else:
            m = s5_layer(h, s5_a_re[j], s5_a_im[j], s5_b_re[j], s5_b_im[j],
                         s5_c_re[j], s5_c_im[j], s5_d[j], s5_log_dt[j], s5_w_glu[j])
        x = x + g2[:, None, :] * m
        h = modulate(rms_norm(x, norm_g[i, 2]), sh3, sc3)
        x = x + 0.5 * g3[:, None, :] * swiglu_ffn(h, ffn_w_in[i, 1], ffn_w_out[i, 1])
    return rms_norm(x, final_g)


_drawn_inputs = setup_inputs


def setup_inputs(seed=0):
    import zlib

    import numpy as np

    out = dict(_drawn_inputs(seed))
    spreads = {}
    factors = {'ada_b': 4.287,
     'norm_g': 5.491,
     's5_a_re': 64.0,
     's5_a_im': 63.312,
     's5_b_re': 64.0,
     's5_b_im': 64.0,
     's5_c_re': 64.0,
     's5_c_im': 64.0,
     's5_log_dt': 64.0,
     'final_g': 8.185}
    for name, (base, spread) in spreads.items():
        noise = np.random.default_rng([zlib.crc32(name.encode()), seed]).standard_normal(out[name].shape)
        drawn = base * np.exp(spread * noise) if base else spread * noise
        out[name] = __import__('jax').numpy.asarray(drawn.astype(out[name].dtype))
    for name, factor in factors.items():
        out[name] = (out[name] * factor).astype(out[name].dtype)
    return out
```

```python
from contextlib import ExitStack, contextmanager

import numpy as np

import concourse.bass as bass
from concourse import mybir

F32 = mybir.dt.float32
F32R = mybir.dt.float32r
I32 = mybir.dt.int32
ALU = mybir.AluOpType
ACT = mybir.ActivationFunctionType

P = 128
D = 1024
L = 512
KT = D // P
TT = L // P
FF = 2816
FT = FF // P
N_MOD = 9
HEADS = 4
DV = 2 * D // HEADS
CW = 256
NORM_EPS = 1e-6
GN_EPS = 1e-5

FFN_PAIRS = FT // 2
FFN_OUT = (8, 8, 6)
RET_OUT = (8, 8)
OUT_PAIRS = KT // 2

C_FFN = [0, 66, 100, 142]
C_RET = 34
C_RET_OUT = C_RET + 6 * HEADS
C_GLU = 134
N_CHUNKS = 176

ADA_W = 512
ADA_FIRST = 4
ADA_IN = FFN_PAIRS - 1
ADA_AT = {0: (0, 10), 1: (14, 24), 2: (None, 28), 3: (None, None)}

G, NS, SK = 64, 64, 16
SC = P // SK
NC = L // SC
GB = P // SK
S5_LEFT = {"ctab": ([P, G, NC], F32), "stab": ([P, G, NC], F32),
           "b_re": ([P, G, SK], F32), "b_im": ([P, G, SK], F32), "c_re": ([P, G, SK], F32),
           "c_im": ([P, G, SK], F32), "pw1": ([P, G, SC + 1], F32), "pw2": ([P, G, SC + 1], F32)}
S5_LOAD = {"b_nat": ([NS, 2, NS * SK], F32), "c_nat": ([P, 2, KT, P], F32), "a_nat": ([NS, 2, P], F32),
           "log_dt": ([P, G], F32)}
S5_TABLE = {"tab_tmp": ([P, G, NC // 2], F32), "bb_tmp": ([P, G, SK], F32)}
S5_WORK = {"xs": ([P, GB, SC, SK], F32), "xt": ([P, GB // 2, SC, SK], F32),
           "ys": ([P, 2, GB, SC + 1, SK], F32), "yt": ([P, GB // 2, SC + 1, SK], F32),
           "zt": ([NS, GB * P], F32), "sp": ([P, GB, NC], F32), "b_rows": ([P, GB, P], F32),
           "mt": ([P, 2, GB, P], F32)}
S5_RIGHT = {"x_again": ([P, KT, L], F32), "win": ([P, GB, P], F32), "us": ([P, 2, GB, NC], F32)}
SMALL = ("are aim dt x th cnt half arg sh ch tn em1 ex w s1 c1 nre nim a b fre fim t1 t2").split()

COL_G = 2 * N_MOD * KT
COL_FG = COL_G + 6 * KT
COL_D = COL_FG + KT
COL_C = COL_D + KT


class Steps:

    def __init__(self, eng, sem):
        self.eng, self.sem, self.n, self.i, self.per = eng, sem, 0, None, 0

    def value(self):
        return self.n if self.i is None else self.i * self.per + self.n

    def __call__(self, ins):
        ins.then_inc(self.sem, 1)
        self.n += 1
        return ins

    def wait(self):
        self.eng.wait_ge(self.sem, self.value())

    @contextmanager
    def loop(self, count, per):
        with self.eng.Fori(0, count) as i:
            start = self.n
            self.i, self.per = i, per
            yield i
            assert self.n - start == per, (self.n - start, per)
            self.i = None
            self.n = start + per * count


def build(nc, ins, out):
    x_d, c_d, pos_d = ins["x"], ins["c"], ins["positions"]
    ctx = ExitStack()
    with ctx:
        def sb(name, shape, dt=F32, **k):
            return ctx.enter_context(nc.sbuf_tensor(name, shape, dt, **k))

        def sem(name):
            return ctx.enter_context(nc.semaphore(name))

        h_hi = sb("h_hi", [P, KT, L], F32R)
        with ExitStack() as shared:
            h_lo = shared.enter_context(nc.sbuf_tensor("h_lo", [P, KT, L], F32R))
        u = sb("u", [P, KT, L])
        w_raw = [sb(f"w_raw{s}", [P, 8, CW]) for s in range(2)]
        w_hi = [sb(f"w_hi{s}", [P, 8, CW], F32R) for s in range(2)]
        w_lo = [sb(f"w_lo{s}", [P, 8, CW], F32R) for s in range(2)]
        s_buf = sb("s_buf", [P, 2, L])
        sq = sb("sq", [P, 2, L])
        acc = sb("acc", [P, L])
        ident = sb("ident", [P, P])
        ones = sb("ones", [P, P])
        mods = sb("mods", [P, 2 * N_MOD * KT])
        par = sb("par", [P, 3 * N_MOD * KT])
        csil = sb("csil", [P, KT])
        scale1 = sb("scale1", [P, KT])
        coef = sb("coef", [P, KT])
        ms = sb("ms", [P, TT])
        rstd = sb("rstd", [P, TT])
        mhalf = sb("mhalf", [P, TT])
        bn = sb("bn", [P, 2, 8])
        gn = sb("gn", [P, 2, 2])
        freq = sb("freq", [P, 1])

        def zone(side, *sets):
            for tensors in sets:
                with ExitStack() as z:
                    for name, (shape, dt) in tensors.items():
                        again = name in T
                        t = z.enter_context(nc.sbuf_tensor(name + f"_{len(T)}" * again, shape, dt, side=side))
                        T.setdefault(name, t)

        T = {}
        zone("left",
             {"g_hi": ([P, FT, L], F32R), "g_lo": ([P, FT, L], F32R)},
             {"x_tok": ([P, TT, D], F32), "ada_first": ([P, ADA_FIRST, KT, ADA_W], F32)},
             {**S5_LEFT, **S5_LOAD}, {**S5_LEFT, **S5_TABLE}, {**S5_LEFT, **S5_WORK})
        hold = ctx.enter_context(nc.sbuf_tensor("hold", [P, 2 * FT * L], F32))
        zone("right",
             {"x_sb": ([P, KT, L], F32), "ada_raw": ([P, 2, 2, ADA_W], F32), "ada_acc": ([P, ADA_W], F32)},
             {"k_hi": ([P, 2, L], F32R), "k_lo": ([P, 2, L], F32R), "sil_g": ([P, TT, L], F32),
              "s_hi": ([P, L], F32R), "s_lo": ([P, L], F32R),
              "cos": ([P, L], F32), "sin": ([P, L], F32), "decay": ([P, L], F32)},
             S5_RIGHT)
        g_hi, g_lo, x_tok, ada_first = T["g_hi"], T["g_lo"], T["x_tok"], T["ada_first"]
        x_sb, ada_raw, ada_acc = T["x_sb"], T["ada_raw"], T["ada_acc"]
        k_hi, k_lo, sil_g, s_hi, s_lo = T["k_hi"], T["k_lo"], T["sil_g"], T["s_hi"], T["s_lo"]
        cos, sin, decay = T["cos"], T["sin"], T["decay"]
        o_n = sq[:, 0, :]
        RT = HEADS * DV // P
        v_hi, v_lo = g_hi[:, RT:RT + TT, :], g_lo[:, RT:RT + TT, :]
        q_hi, q_lo = g_hi[:, RT + TT:RT + TT + 2, :], g_lo[:, RT + TT:RT + TT + 2, :]
        slots = [s_buf[:, 0], s_buf[:, 1], sq[:, 0], sq[:, 1]]
        x_spill = nc.dram_tensor("x_spill", [P, KT, L], F32, kind="Internal").ap()

        ps = ctx.enter_context(nc.psum_tensor("ps", [P, 8, L], F32))

        w_landed = [sem(f"w_landed{s}") for s in range(2)]
        w_hi_done, w_lo_done, w_used = sem("w_hi_done"), sem("w_lo_done"), sem("w_used")
        consts, rows_in, x_in = sem("consts"), sem("rows_in"), [sem(f"x_in{t}") for t in range(TT)]
        ada0_in = [sem(f"ada0_in{q}") for q in range(ADA_FIRST)]
        rows_turned, par_done, csil_done = sem("rows_turned"), sem("par_done"), sem("csil_done")
        x_turned, x_copied = sem("x_turned"), sem("x_copied")
        ada_landed = [sem(f"ada_landed{s}") for s in range(2)]
        ada_used, ada_acc_done, ada_summed, mods_done = (
            sem("ada_used"), sem("ada_acc_done"), sem("ada_summed"), sem("mods_done"))
        x_done, sq_done, acc_done, stat_done = sem("x_done"), sem("sq_done"), sem("acc_done"), sem("stat_done")
        ms_done, rstd_done, diag_done, rbc_done = sem("ms_done"), sem("rstd_done"), sem("diag_done"), sem("rbc_done")
        xn_done, hf_done, h_hi_done, h_lo_done = sem("xn_done"), sem("hf_done"), sem("h_hi_done"), sem("h_lo_done")
        silu_done, prod_done, g_hi_done, g_lo_done = (
            sem("silu_done"), sem("prod_done"), sem("g_hi_done"), sem("g_lo_done"))
        spill_done, back_done = sem("spill_done"), sem("back_done")
        y_turned, y_copied, stored = sem("y_turned"), sem("y_copied"), sem("stored")
        dve_steps, act_steps = sem("dve_steps"), sem("act_steps")
        ang_done, trig_done, rot_in = sem("ang_done"), sem("trig_done"), sem("rot_in")
        rot_done, rot_hi_done, rot_lo_done = sem("rot_done"), sem("rot_hi_done"), sem("rot_lo_done")
        sil_g_done = sem("sil_g_done")
        v_hi_done, v_lo_done = sem("v_hi_done"), sem("v_lo_done")
        score_done, masked, s_hi_done, s_lo_done = sem("score_done"), sem("masked"), sem("s_hi_done"), sem("s_lo_done")
        pv_done, gn_var, gn_rstd, o_normed = sem("pv_done"), sem("gn_var"), sem("gn_rstd"), sem("o_normed")
        o_turned, gated, a_hi_done, a_lo_done = sem("o_turned"), sem("gated"), sem("a_hi_done"), sem("a_lo_done")
        decay_in, bn_ready = sem("decay_in"), sem("bn_ready")

        s5_const = sb("s5_const", [P, 3 + NC])
        sgn, even, odd, cmask = s5_const[:, 0:1], s5_const[:, 1:2], s5_const[:, 2:3], s5_const[:, 3:3 + NC]
        rho = sb("rho", [P, G])
        small = {n: (sq if r < 16 else acc)[:].rearrange("p a n -> p (a n)" if r < 16 else "p n -> p n")[
                     :, (r % 16) * G:(r % 16 + 1) * G] for r, n in enumerate(SMALL)}
        ctab, stab, pw1, pw2 = T["ctab"], T["stab"], T["pw1"], T["pw2"]
        b_re, b_im, c_re, c_im = T["b_re"], T["b_im"], T["c_re"], T["c_im"]
        b_nat, c_nat, a_nat, log_dt = T["b_nat"], T["c_nat"], T["a_nat"], T["log_dt"]
        tab_tmp, bb_tmp = T["tab_tmp"], T["bb_tmp"]
        xs, xt, ys, yt, zt, s_prev = T["xs"], T["xt"], T["ys"], T["yt"], T["zt"], T["sp"]
        win, mt, us = T["win"], T["mt"], T["us"]
        b_rows = T["b_rows"]
        nat_in, dt_in, nat_turned = sem("nat_in"), sem("dt_in"), sem("nat_turned")
        a_copied, nat_copied = sem("a_copied"), sem("nat_copied")
        exp_in, exp_done, wave_in, wave_done = sem("exp_in"), sem("exp_done"), sem("wave_in"), sem("wave_done")
        tabs_done, zeroed = sem("tabs_done"), sem("zeroed")
        (ub_done, u_turned, z_done, z_turned, us_done, xs_step, xs_done, xs_turned, win_done, ys_done, lag_done,
         m_early, m_done, v_done, sp_done, y_done, yz_done, yz_turned, yd_done, gelu_done, a5_hi, a5_lo, gate_done, rows_done, pe_passed
         ) = (sem("s5_" + n) for n in (
             "ub u_turned z z_turned us xs_step xs xs_turned win ys lag m_early m v sp y yz yz_turned yd gelu "
             "hi lo gate b_rows pe_passed").split())

        def raw_f32(ap):
            return ap.bitcast(F32)

        def rows(w):
            return w.rearrange("(t p) n -> p t n", p=P)

        ffn_in = [rows(ins["ffn_w_in"][f // 2, f % 2]) for f in range(4)]
        ffn_out = [rows(ins["ffn_w_out"][f // 2, f % 2]) for f in range(4)]
        ret_in, ret_out = rows(ins["ret_w_in"][0]), rows(ins["ret_w_out"][0])
        glu_w = rows(ins["s5_w_glu"][0])
        ada_w = [rows(ins["ada_w"][l]) for l in range(2)]

        block = ctx.enter_context(nc.Block())

        @block.sync
        def _(sp):
            def load(n, k, src, first=False):
                if not first:
                    sp.wait_ge(w_lo_done, n)
                sp.dma_start(w_raw[k % 2][:, 0:src.shape[1], :], src).then_inc(w_landed[k % 2], 16)

            def load_ada(Q, l, q):
                for p in range(4):
                    sp.wait_ge(ada_used, Q * 4 + (p + 1))
                    src = ada_w[l][:, 2 * p:2 * p + 2, bass.ds(q * ADA_W, ADA_W)]
                    sp.dma_start(ada_raw[:, p % 2], src).then_inc(ada_landed[p % 2], 16)

            def ffn(f):
                n0 = C_FFN[f]
                a_in, a_out = ADA_AT[f]
                def q_of(Q):
                    return (0, Q + ADA_FIRST) if f == 0 else (1, Q - 14)

                def in_pair(i, n, first, ada):
                    load(n, 0, ffn_in[f][:, :, bass.ds(i * CW, CW)], first)
                    load(n + 1, 1, ffn_in[f][:, :, bass.ds(i * CW + FF, CW)], first)
                    if ada:
                        load_ada(i + a_in, *q_of(i + a_in))
                if f == 0:
                    in_pair(0, 0, True, True)
                with sp.Fori(1 if f == 0 else 0, ADA_IN) as i:
                    in_pair(i, i * 2 + n0, False, a_in is not None)
                in_pair(ADA_IN, n0 + 2 * ADA_IN, False, False)
                with sp.Fori(0, 2) as j:
                    n, k = j * 6 + (n0 + 2 * FFN_PAIRS), 0
                    for dp in range(2):
                        for c, r in enumerate(FFN_OUT):
                            load(n + k, k, ffn_out[f][:, 8 * c:8 * c + r, bass.ds(j * 2 * CW + dp * CW, CW)])
                            k += 1
                        if a_out is not None:
                            Q = j * 2 + (a_out + dp)
                            load_ada(Q, *q_of(Q))

            def retention():
                def head_chunk(h, k):
                    at = (h * CW, h * CW + D, h * DV + 4 * D, h * DV + (4 * D + CW),
                          h * DV + 2 * D, h * DV + (2 * D + CW))[k]
                    load(h * 6 + (C_RET + k), k, ret_in[:, :, bass.ds(at, CW)])

                def out_chunk(dp, k):
                    m = len(RET_OUT)
                    c = k % m
                    load(dp * m + C_RET_OUT + c, c, ret_out[:, 8 * c:8 * c + 8, bass.ds(dp * CW, CW)])

                def head(h):
                    head_chunk(h, 2)
                    head_chunk(h, 3)
                    sp.wait_ge(masked, h * TT + 1)
                    sp.dma_start(decay[:], ins["decay"][bass.ds(h, 1), :, :].rearrange("a p n -> (a p) n")
                                 ).then_inc(decay_in, 16)
                    head_chunk(h, 4)
                    head_chunk(h, 5)

                head_chunk(0, 0)
                head_chunk(0, 1)
                sp.wait_ge(x_done, 1 + 2 * OUT_PAIRS)
                sp.dma_start(x_spill, x_sb[:]).then_inc(spill_done, 16)
                sp.wait_ge(xn_done, 1 + 2 * KT)
                sp.wait_ge(spill_done, 16)
                sp.dma_start(freq[:], ins["inv_freq"]).then_inc(rot_in, 16)
                sp.dma_start(cos[:].bitcast(I32), pos_d.broadcast_to([P, L])).then_inc(rot_in, 16)
                with sp.Fori(0, HEADS - 1) as h:
                    head(h)
                    head_chunk(h + 1, 0)
                    head_chunk(h + 1, 1)
                head(HEADS - 1)
                out_chunk(0, 0)
                out_chunk(0, 1)
                sp.wait_ge(a_lo_done, 1 + HEADS * TT)
                sp.dma_start(x_sb[:], x_spill).then_inc(back_done, 16)
                with sp.Fori(1, OUT_PAIRS) as dp:
                    out_chunk(dp, 0)
                    out_chunk(dp, 1)

            def s5():
                def glu_pair(i, dp0):
                    for k in range(2):
                        load(i * 2 + (C_GLU + 2 * dp0 + k), k, glu_w[:, :, bass.ds(i * CW + (dp0 * CW + (D, 0)[k]), CW)])
                glu_pair(0, 0)
                sp.wait_ge(x_done, 1 + 5 * OUT_PAIRS)
                for r, name in enumerate(("s5_a_re", "s5_a_im")):
                    for half in range(2):
                        sp.dma_start(a_nat[:, r, half * NS:(half + 1) * NS], ins[name][0]).then_inc(nat_in, 16)
                sp.dma_start(log_dt[:], ins["s5_log_dt"].broadcast_to([P, G])).then_inc(dt_in, 16)
                for r, name in enumerate(("s5_b_re", "s5_b_im")):
                    sp.dma_start(b_nat[:, r], ins[name][0].rearrange("g p k -> g (p k)")).then_inc(nat_in, 16)
                for r, name in enumerate(("s5_c_re", "s5_c_im")):
                    src = ins[name][0].rearrange("(b g) k p -> (g k) b p", g=GB)
                    for half in range(2):
                        sp.dma_start(c_nat[:, r, :, half * NS:(half + 1) * NS], src).then_inc(nat_in, 16)
                with sp.Fori(0, OUT_PAIRS - 1) as i:
                    glu_pair(i, 1)

            sp.dma_start(s5_const[:], ins["s5_const"]).then_inc(rows_in, 16)
            sp.dma_start(sq[0:72, 0, 0:P], ins["ada_b"][0].rearrange("(r n) -> r n", n=P)).then_inc(rows_in, 16)
            sp.dma_start(sq[0:72, 0, P:2 * P], ins["ada_b"][1].rearrange("(r n) -> r n", n=P)).then_inc(rows_in, 16)
            at = 0
            for src in (ins["norm_g"].rearrange("l s (r n) -> (l s r) n", n=P),
                        ins["final_g"].rearrange("(r n) -> r n", n=P),
                        ins["s5_d"].rearrange("l (r n) -> (l r) n", n=P),
                        c_d.rearrange("b (r n) -> (b r) n", n=P)):
                sp.dma_start(sq[at:at + src.shape[0], 0, 2 * P:3 * P], src).then_inc(rows_in, 16)
                at += src.shape[0]
            for q in range(ADA_FIRST):
                for half in range(2):
                    sp.dma_start(ada_first[:, q, 4 * half:4 * half + 4, :],
                                 ada_w[0][:, 4 * half:4 * half + 4, q * ADA_W:(q + 1) * ADA_W]
                                 ).then_inc(ada0_in[q], 16)
            ffn(0)
            retention()
            ffn(1)
            ffn(2)
            s5()
            ffn(3)
            sp.wait_ge(y_copied, KT)
            out_v = out.rearrange("b (t p) n -> p (b t) n", p=P)
            sp.dma_start(out_v, x_tok[:]).then_inc(stored, 16)
            sp.wait_ge(stored, 16)

        @block.gpsimd
        def _(pool):
            nc.gpsimd.memset(ident[:], 0.0).then_inc(consts, 1)
            nc.gpsimd.memset(ones[:], 1.0).then_inc(consts, 1)
            nc.gpsimd.memset(mhalf[:], -0.5).then_inc(consts, 1)
            pool.wait_ge(consts, 3)
            nc.gpsimd.affine_select(out=ident[:], in_=ident[:], compare_op=ALU.not_equal, fill=1.0, base=0,
                                    pattern=[[-1, P]], channel_multiplier=1).then_inc(consts, 1)

            def norm(k):
                pool.wait_ge(ms_done, k + 1)
                nc.gpsimd.tensor_tensor(rstd[:], ms[:], mhalf[:], ALU.pow).then_inc(rstd_done, 1)

            def retention():
                with pool.Fori(0, HEADS) as h:
                    for I in range(TT):
                        pool.wait_ge(gn_var, h * TT + (I + 1))
                        nc.gpsimd.tensor_tensor(gn[:, I % 2, 1:2], gn[:, I % 2, 0:1], mhalf[:, 0:1],
                                                ALU.pow).then_inc(gn_rstd, 1)
            def s5():
                ebase, g = rho, nc.gpsimd
                g.memset(rho[:], float(np.e)).then_inc(zeroed, 1)
                pool.wait_ge(zeroed, 1)
                pool.wait_ge(dt_in, 16)
                pool.wait_ge(exp_in, 1)
                g.tensor_tensor(small["dt"], rho[:], log_dt[:], ALU.pow).then_inc(exp_done, 1)
                pool.wait_ge(exp_in, 2)
                pool.wait_ge(exp_done, 1)
                g.tensor_tensor(rho[:], rho[:], small["t1"], ALU.pow).then_inc(exp_done, 1)
                pool.wait_ge(tabs_done, 1)
                g.memset(s_prev[:], 0.0).then_inc(zeroed, 1)
                g.memset(mt[:], 0.0).then_inc(zeroed, 1)
                g.sem_inc(xs_step, 1)
                def inputs_powers(b):
                    if not (isinstance(b, int) and b == 0):
                        pool.wait_ge(xs_turned, b)
                        pool.wait_ge(rows_done, b)
                    for hf in range(2):
                        gs = bass.ds(b * GB + hf * (GB // 2), GB // 2)
                        shape = [P, GB // 2, SC, SK]
                        xh = xs[:, hf * (GB // 2):(hf + 1) * (GB // 2)]
                        pool.wait_ge(xs_step, b * 6 + (3 * hf + 1))
                        g.tensor_tensor(xh, b_re[:, gs, :].unsqueeze(2).broadcast_to(shape),
                                        pw1[:, gs, 0:SC].unsqueeze(3).broadcast_to(shape),
                                        ALU.mult).then_inc(xs_step, 1)
                        g.tensor_tensor(xt[:], b_im[:, gs, :].unsqueeze(2).broadcast_to(shape),
                                        pw2[:, gs, 0:SC].unsqueeze(3).broadcast_to(shape),
                                        ALU.mult).then_inc(xs_step, 1)
                        pool.wait_ge(xs_step, b * 6 + (3 * hf + 3))
                        g.tensor_tensor(xh, xh, xt[:], ALU.add).then_inc(xs_step, 1)
                    pool.wait_ge(xs_step, b * 6 + 7)
                    g.sem_inc(xs_done, 1)

                inputs_powers(0)
                with pool.Fori(1, KT) as b:
                    inputs_powers(b)

            norm(0)
            norm(1)
            retention()
            norm(2)
            norm(3)
            norm(4)
            s5()
            norm(5)
            norm(6)

        @block.scalar
        def _(act):
            st = Steps(act, act_steps)
            copy = lambda o, i: nc.scalar.activation(o, i, ACT.Copy)

            def split_hi(n, k, r=8):
                act.wait_ge(w_landed[k % 2], landed(n, k))
                act.wait_ge(w_used, n)
                copy(w_hi[k % 2][:, 0:r, :], w_raw[k % 2][:, 0:r, :]).then_inc(w_hi_done, 1)

            def norm(k, shift, plain=None):
                for t in range(KT):
                    act.wait_ge(xn_done, 1 + KT * k + t + 1)
                    if plain is None:
                        nc.scalar.activation(slots[t % 4], slots[t % 4], ACT.Identity,
                                             bias=mods[:, shift + t:shift + t + 1],
                                             scale=scale1[:, t:t + 1]).then_inc(hf_done, 1)
                        act.wait_ge(hf_done, KT * k + t + 1)
                        copy(h_hi[:, t], slots[t % 4]).then_inc(h_hi_done, 1)
                    elif plain == "u":
                        nc.scalar.activation(u[:, t], slots[t % 4], ACT.Identity,
                                             bias=mods[:, shift + t:shift + t + 1],
                                             scale=scale1[:, t:t + 1]).then_inc(hf_done, 1)
                    else:
                        nc.scalar.activation(slots[t % 4], slots[t % 4], ACT.Identity,
                                             scale=par[:, COL_FG + t:COL_FG + t + 1]).then_inc(hf_done, 1)
                        act.wait_ge(y_turned, t + 1)
                        copy(x_tok[:, :, t * P:(t + 1) * P],
                             ps[:, t % 2, :].rearrange("p (t n) -> p t n", t=TT)).then_inc(y_copied, 1)

            def square(pair, tiles):
                act.wait_ge(x_done, pair + 2)
                act.wait_ge(acc_done, pair + 1)
                nc.scalar.activation(sq[:], x_sb[:, tiles, :], ACT.Square).then_inc(sq_done, 1)

            def out_phase(n0, chunks, pair0, last=False):
                m = len(chunks)
                def body(j, last):
                    n = j * (2 * m) + n0
                    for dp in range(2):
                        for c in range(m):
                            k = dp * m + c
                            if not (last and k == 2 * m - 1):
                                nr = chunks[(c + 1) % m]
                                split_hi(n + (k + 1), k + 1, nr)
                        square(j * 2 + (pair0 + dp), bass.ds(j * 4 + 2 * dp, 2))
                if last:
                    body(0, False)
                    body(1, True)
                else:
                    with act.Fori(0, 2) as j:
                        body(j, False)

            def ffn(f, last=False):
                n0 = C_FFN[f]
                def in_pair(i):
                    n = i * 2 + n0
                    split_hi(n + 1, 1)
                    act.wait_ge(w_used, n + 2)
                    act.wait_ge(g_lo_done, i + (FFN_PAIRS * f + 1))
                    nc.scalar.activation(s_buf[:], ps[:, 0:2], ACT.Silu).then_inc(silu_done, 1)
                    split_hi(n + 2, 0)
                    act.wait_ge(prod_done, i + (FFN_PAIRS * f + 2))
                    copy(g_hi[:, bass.ds(i * 2, 2), :], s_buf[:]).then_inc(g_hi_done, 1)
                with act.Fori(0, ADA_IN) as i:
                    in_pair(i)
                in_pair(ADA_IN)
                out_phase(n0 + 2 * FFN_PAIRS, FFN_OUT, OUT_PAIRS * (SUB[f] + 1), last)

            def retention():
                act.wait_ge(ang_done, 1)
                nc.scalar.activation(sin[:], sq[:, 0], ACT.Sin).then_inc(trig_done, 1)
                nc.scalar.activation(cos[:], sq[:, 1], ACT.Sin).then_inc(trig_done, 1)
                with act.Fori(0, HEADS) as h:
                    n = h * 6 + C_RET
                    for k in range(6):
                        split_hi(n + (k + 1), k + 1)
                        if k < 2:
                            act.wait_ge(rot_done, h * 2 + (k + 1))
                            dst = (q_hi, k_hi)[k]
                            copy(dst[:, 0:2, :], s_buf[:]).then_inc(rot_hi_done, 1)
                        elif k < 4:
                            act.wait_ge(w_used, n + (k + 2))
                            if k == 2:
                                act.wait_ge(a_lo_done, h * TT + 1)
                            nc.scalar.activation(sil_g[:, 2 * (k - 2):2 * (k - 2) + 2, :],
                                                 ps[:, 4 + 2 * (k - 2):6 + 2 * (k - 2)], ACT.Silu
                                                 ).then_inc(sil_g_done, 1)
                        else:
                            if k == 5:
                                scores_hi(h, 0)
                            act.wait_ge(w_used, n + (k + 2))
                            e = (k - 4) * CW
                            copy(v_hi[:, :, e:e + CW],
                                 ps[:, 2 * (k - 4):2 * (k - 4) + 2].rearrange("p b (t n) -> p (b t) n", t=2)
                                 ).then_inc(v_hi_done, 1)
                    for I in range(TT):
                        if I + 1 < TT:
                            scores_hi(h, I + 1)
                        act.wait_ge(gated, h * TT + (I + 1))
                        copy(g_hi[:, bass.ds(h * TT, TT), I * P:(I + 1) * P],
                             s_buf[:, 0].rearrange("p (t n) -> p t n", t=TT)).then_inc(a_hi_done, 1)

            def scores_hi(h, I):
                act.wait_ge(masked, h * TT + (I + 2))
                W = (I + 1) * P
                copy(s_hi[:, 0:W], s_buf[:, 1, 0:W]).then_inc(s_hi_done, 1)

            def s5():
                A = nc.scalar.activation
                for r, t in enumerate((b_re, b_im)):
                    act.wait_ge(nat_turned, r + 2)
                    for half in range(2):
                        ins = copy(t[half * NS:(half + 1) * NS],
                                   ps[0:NS, 2 * r:2 * r + 2].rearrange("p a (k g) -> p g (a k)", g=G))
                    ins.then_inc(nat_copied, 1)
                for r, t in enumerate((c_re, c_im)):
                    act.wait_ge(nat_turned, r + 4)
                    A(t[:].rearrange("p g k -> p (g k)"), ps[:, 4 + 2 * r:6 + 2 * r].rearrange("p a n -> p (a n)"),
                      ACT.Identity, scale=sgn).then_inc(nat_copied, 1)
                act.wait_ge(wave_in, 1)
                A(small["sh"], small["half"], ACT.Sin)
                A(small["ch"], small["arg"], ACT.Sin)
                A(small["tn"], small["x"], ACT.Tanh, scale=0.5).then_inc(wave_done, 1)
                act.wait_ge(tabs_done, 1)
                act.sem_inc(yz_done, 1)

                def tokens(b, first=False):
                    if not first:
                        act.wait_ge(u_turned, b)
                    copy(s_buf[:, 1], u[:, bass.ds(b, 1), :].rearrange("p a n -> p (a n)")).then_inc(ub_done, 1)
                    act.wait_ge(xs_done, b + 1)
                    if not first:
                        act.wait_ge(lag_done, b)
                    copy(b_rows[:].rearrange("p g (j k) -> p g j k", k=SK),
                         xs[:, :, 0:1, :].broadcast_to([P, GB, SC, SK])).then_inc(rows_done, 1)

                def front(b, s, first=False):
                    act.wait_ge(u_turned, b + 1)
                    if not first:
                        act.wait_ge(yz_turned, b)
                    copy(zt[:].rearrange("c (g j k) -> c j g k", g=GB, j=SC),
                         ps[0:NC, 0:2].rearrange("c a (j g k) -> c (a j) g k", g=GB, k=SK)).then_inc(z_done, 1)
                    act.wait_ge(xs_turned, b + 1)
                    if not first:
                        act.wait_ge(v_done, b)
                    copy(win[:].rearrange("p g n -> p (g n)"), ps[:, 3:5].rearrange("p a n -> p (a n)")
                         ).then_inc(win_done, 1)
                    act.wait_ge(lag_done, b + 1)
                    if not first:
                        act.wait_ge(y_done, b)
                    for J in range(4):
                        q = slice(32 * J, 32 * J + 32)
                        w = (2 * J + 2) * SK
                        ins = A(mt[q, s, :, P - w:P], ps[q, 5:7].rearrange("p a (g n) -> p (a g) n", n=P)[:, :, 0:w],
                                ACT.Copy, scale=odd[q])
                    ins.then_inc(m_early, 1)

                def back(b, after=False):
                    act.wait_ge(y_done, b + 2)
                    copy(zt[:].rearrange("c (i g k) -> c g i k", g=GB, i=SC),
                         ps[0:NC, 0:2].rearrange("c a (g i k) -> c (a g) i k", i=SC, k=SK)).then_inc(yz_done, 1)
                    if after:
                        tokens(b + 2)
                    act.wait_ge(yd_done, b + 2)
                    A(s_buf[:, 0], s_buf[:, 0], ACT.Gelu_apprx_tanh).then_inc(gelu_done, 1)
                    act.wait_ge(gelu_done, b + 1)
                    copy(h_hi[:, bass.ds(b, 1), :].rearrange("p a n -> p (a n)"), s_buf[:, 0]).then_inc(a5_hi, 1)

                tokens(0, True)
                front(0, 0, True)
                tokens(1)
                with act.Fori(0, KT // 2 - 1) as i:
                    for s in range(2):
                        front(i * 2 + (s + 1), 1 - s)
                        back(i * 2 + s, True)
                front(KT - 1, 1)
                back(KT - 2)
                back(KT - 1)
                with act.Fori(0, OUT_PAIRS) as dp:
                    n = dp * 2 + C_GLU
                    split_hi(n + 1, 1)
                    act.wait_ge(w_used, n + 2)
                    act.wait_ge(x_done, dp + (5 * OUT_PAIRS + 1))
                    A(s_buf[:], ps[:, 0:2], ACT.Sigmoid).then_inc(gate_done, 1)
                    split_hi(n + 2, 0)
                    square(dp + 5 * OUT_PAIRS, bass.ds(dp * 2, 2))

            act.sem_inc(w_hi_done, 1)
            act.sem_inc(silu_done, 1)
            for t in range(TT):
                act.dma_start(x_tok[:, t], x_d[0].rearrange("(t p) n -> p t n", p=P)[:, t]).then_inc(x_in[t], 16)
            act.wait_ge(par_done, 1)
            nc.scalar.activation(csil[:], par[:, COL_C:COL_C + KT], ACT.Silu).then_inc(csil_done, 1)
            for pr in range(OUT_PAIRS):
                act.wait_ge(x_turned, 2 * pr + 2)
                copy(x_sb[:, 2 * pr:2 * pr + 2], ps[:, (2 * pr) % 4:(2 * pr) % 4 + 2]).then_inc(x_copied, 1)
                act.wait_ge(x_copied, pr + 1)
                if pr:
                    act.wait_ge(acc_done, pr + 1)
                nc.scalar.activation(sq[:], x_sb[:, 2 * pr:2 * pr + 2], ACT.Square).then_inc(sq_done, 1)
            act.wait_ge(w_landed[0], 16)
            copy(w_hi[0][:], w_raw[0][:]).then_inc(w_hi_done, 1)
            norm(0, 0)
            ffn(0)
            norm(1, 3 * KT)
            retention()
            out_phase(C_RET_OUT, RET_OUT, OUT_PAIRS * 2)
            norm(2, 6 * KT)
            ffn(1)
            norm(3, 9 * KT)
            ffn(2)
            norm(4, 12 * KT, "u")
            s5()
            norm(5, 15 * KT)
            ffn(3, True)
            norm(6, 0, "out")

        @block.vector
        def _(dve):
            st = Steps(dve, dve_steps)
            V = nc.vector

            def split_lo(n, k, r=8):
                dve.wait_ge(w_hi_done, n + 2)
                V.tensor_tensor(w_lo[k % 2][:, 0:r, :], w_raw[k % 2][:, 0:r, :],
                                raw_f32(w_hi[k % 2][:, 0:r, :]), ALU.subtract).then_inc(w_lo_done, 1)

            def ada_terms(raw, c0, into, first):
                for t in range(raw.shape[1]):
                    c = csil[:, c0 + t:c0 + t + 1]
                    if first and t == 0:
                        st(V.tensor_scalar(into, raw[:, t], c, None, ALU.mult))
                    else:
                        st.wait()
                        st(V.scalar_tensor_tensor(out=into, in0=raw[:, t], scalar=c, in1=into,
                                                  op0=ALU.mult, op1=ALU.add))

            def ada_step(Q):
                dve.wait_ge(ada_summed, Q + ADA_FIRST)
                for p in range(4):
                    dve.wait_ge(ada_landed[p % 2], Q * 32 + (16 + 16 * (p // 2)))
                    ada_terms(ada_raw[:, p % 2], 2 * p, ada_acc[:], p == 0)
                    st.wait()
                    dve.sem_inc(ada_used, 1)
                dve.sem_inc(ada_acc_done, 1)

            def ada_bias(Q):
                dve.wait_ge(ada_summed, Q + (ADA_FIRST + 1))
                at = bass.ds(Q * 4 + 4 * ADA_FIRST, 4)
                V.tensor_tensor(mods[:, at], ps[:, 6, 0:4], par[:, at], ALU.add).then_inc(mods_done, 1)

            def add_squares(pair):
                dve.wait_ge(sq_done, pair + 1)
                for t in range(2):
                    st.wait()
                    ins = st(V.tensor_tensor(acc[:], acc[:], sq[:, t], ALU.add))
                st.wait()
                dve.sem_inc(acc_done, 1)

            def norm(k, l, s, kind="h"):
                if kind != "out":
                    dve.wait_ge(mods_done, MODS_NEED[k])
                    c = (l * N_MOD + 3 * s + 1) * KT
                    g = COL_G + (3 * l + s) * KT
                    V.scalar_tensor_tensor(out=scale1[:], in0=mods[:, c:c + KT], scalar=1.0, in1=par[:, g:g + KT],
                                           op0=ALU.add, op1=ALU.mult)
                dve.wait_ge(stat_done, k + 1)
                V.tensor_scalar(ms[:], ps[:, 4, 0:TT], 1.0 / D, NORM_EPS, ALU.mult, ALU.add).then_inc(ms_done, 1)
                dve.wait_ge(rstd_done, k + 1)
                V.tensor_tensor(sq[:, 0, :].rearrange("p (t n) -> p t n", t=TT),
                                ident[:].rearrange("p (a n) -> p a n", a=1).broadcast_to([P, TT, P]),
                                rstd[:].rearrange("p (t a) -> p t a", a=1).broadcast_to([P, TT, P]),
                                ALU.mult).then_inc(diag_done, 1)
                st(V.memset(acc[:], 0.0))
                dve.wait_ge(rbc_done, k + 1)

                def lo(t):
                    dve.wait_ge(h_hi_done, HK[k] * KT + t + 1)
                    V.tensor_tensor(h_lo[:, t], slots[t % 4], raw_f32(h_hi[:, t]),
                                    ALU.subtract).then_inc(h_lo_done, 1)
                for t in range(KT):
                    if t >= 2:
                        if kind == "h":
                            lo(t - 2)
                    if t >= 4:
                        if kind == "h":
                            dve.wait_ge(h_lo_done, HK[k] * KT + t - 3)
                        elif kind == "u":
                            dve.wait_ge(hf_done, KT * k + t - 3)
                        else:
                            dve.wait_ge(y_turned, t - 3)
                    V.tensor_tensor(slots[t % 4], x_sb[:, t], ps[:, 5], ALU.mult).then_inc(xn_done, 1)
                if kind == "h":
                    lo(KT - 2)
                    lo(KT - 1)

            def set_coef(l, s, factor, need):
                dve.wait_ge(mods_done, need)
                c = (l * N_MOD + 3 * s + 2) * KT
                st(V.tensor_scalar(coef[:], mods[:, c:c + KT], factor, None, ALU.mult))

            def residual(j, dp, banks):
                st.wait()
                for t in range(2):
                    tile = bass.ds(j * 4 + (2 * dp + t), 1)
                    ins = V.scalar_tensor_tensor(out=x_sb[:, tile, :], in0=ps[:, banks + t:banks + t + 1, :],
                                                 scalar=coef[:, tile], in1=x_sb[:, tile, :],
                                                 op0=ALU.mult, op1=ALU.add)
                ins.then_inc(x_done, 1)

            def out_phase(n0, chunks, pair0, last=False, ada=None):
                m = len(chunks)
                def body(j, last):
                    n = j * (2 * m) + n0
                    for dp in range(2):
                        for c in range(m):
                            k = dp * m + c
                            if not (last and k == 2 * m - 1):
                                split_lo(n + (k + 1), k + 1, chunks[(c + 1) % m])
                            if ada is not None and c == 1:
                                ada_step(j * 2 + (ada + dp))
                        dve.wait_ge(w_used, n + (k + 2))
                        residual(j, dp, 2 * dp)
                        if ada is not None:
                            ada_bias(j * 2 + (ada + dp))
                        add_squares(j * 2 + (pair0 + dp))
                per = 4 + (16 if ada is not None else 0)
                if last:
                    body(0, False)
                    body(1, True)
                else:
                    with st.loop(2, per) as j:
                        body(j, False)

            def ffn(f, last=False):
                n0 = C_FFN[f]
                a_in, a_out = ADA_AT[f]
                def in_pair(i, ada):
                    n = i * 2 + n0
                    split_lo(n + 1, 1)
                    if ada:
                        ada_step(i + a_in)
                    split_lo(n + 2, 0)
                    dve.wait_ge(w_used, n + 3)
                    dve.wait_ge(silu_done, i + (FFN_PAIRS * f + 2))
                    V.tensor_tensor(s_buf[:], s_buf[:], ps[:, 2:4], ALU.mult).then_inc(prod_done, 1)
                    if ada:
                        ada_bias(i + a_in)
                    dve.wait_ge(g_hi_done, i + (FFN_PAIRS * f + 1))
                    V.tensor_tensor(g_lo[:, bass.ds(i * 2, 2), :], s_buf[:], raw_f32(g_hi[:, bass.ds(i * 2, 2), :]),
                                    ALU.subtract).then_inc(g_lo_done, 1)
                ada = a_in is not None
                with st.loop(ADA_IN, 8 if ada else 0) as i:
                    in_pair(i, ada)
                in_pair(ADA_IN, False)
                set_coef(f // 2, 2 * (f % 2), 0.5, (14, 28, 32, 36)[f])
                out_phase(n0 + 2 * FFN_PAIRS, FFN_OUT, OUT_PAIRS * (SUB[f] + 1), last, a_out)

            def reduce_turns(ang, cnt):
                turn, magic = 2 * np.pi, 1.5 * 2.0 ** 23
                parts, rest = [], turn
                for bits in (5, 13, 21):
                    parts.append(float(np.floor(rest * 2.0 ** bits) / 2.0 ** bits))
                    rest -= parts[-1]
                parts.append(float(np.float32(rest)))
                st(V.tensor_scalar(cnt, ang, 1.0 / turn, None, ALU.mult))
                st.wait()
                st(V.tensor_scalar(cnt, cnt, magic, None, ALU.add))
                st.wait()
                st(V.tensor_scalar(cnt, cnt, magic, None, ALU.subtract))
                st.wait()
                for part in parts:
                    st(V.scalar_tensor_tensor(out=ang, in0=cnt, scalar=-part, in1=ang, op0=ALU.mult, op1=ALU.add))
                    st.wait()
                lim = float(np.nextafter(np.float32(np.pi), np.float32(0)))
                st(V.tensor_scalar(ang, ang, lim, -lim, ALU.min, ALU.max))
                st.wait()

            def angles():
                dve.wait_ge(rot_in, 32)
                posf, ang, cnt = s_buf[:, 0], sq[:, 0], s_buf[:, 1]
                st(V.tensor_copy(posf, cos[:].bitcast(I32)))
                st.wait()
                st(V.tensor_scalar(ang, posf, freq[:], None, ALU.mult))
                st.wait()
                reduce_turns(ang, cnt)
                st(V.tensor_scalar(sq[:, 1], ang, -1.0, None, ALU.mult))
                st.wait()
                st(V.tensor_tensor(sq[:, 1], sq[:, 1], ang, ALU.min))
                st.wait()
                V.tensor_scalar(sq[:, 1], sq[:, 1], float(np.float32(np.pi / 2)), None, ALU.add).then_inc(ang_done, 1)

            def retention():
                angles()
                dve.wait_ge(trig_done, 2)
                with st.loop(HEADS, 12 + 8) as h:
                    n = h * 6 + C_RET
                    for k in range(6):
                        split_lo(n + (k + 1), k + 1)
                        if k < 2:
                            dve.wait_ge(w_used, n + (k + 2))
                            t1, t2 = ps[:, 2 * k], ps[:, 2 * k + 1]
                            st.wait()
                            st(V.tensor_tensor(sq[:, 0], t1, cos[:], ALU.mult))
                            st(V.tensor_tensor(sq[:, 1], t2, sin[:], ALU.mult))
                            dve.wait_ge(rot_lo_done, h * 2 + (k + 1))
                            st(V.tensor_tensor(s_buf[:, 1], t1, sin[:], ALU.mult))
                            st.wait()
                            st(V.tensor_tensor(s_buf[:, 0], sq[:, 0], sq[:, 1], ALU.subtract))
                            st.wait()
                            st(V.tensor_tensor(sq[:, 0], t2, cos[:], ALU.mult))
                            st.wait()
                            st(V.tensor_tensor(s_buf[:, 1], s_buf[:, 1], sq[:, 0], ALU.add))
                            st.wait()
                            dve.sem_inc(rot_done, 1)
                            dve.wait_ge(rot_hi_done, h * 2 + (k + 1))
                            hi, lo = ((q_hi, q_lo), (k_hi, k_lo))[k]
                            V.tensor_tensor(lo[:, 0:2, :], s_buf[:], raw_f32(hi[:, 0:2, :]),
                                            ALU.subtract).then_inc(rot_lo_done, 1)
                        elif k >= 4:
                            if k == 5:
                                scores_masked(h, 0)
                            dve.wait_ge(v_hi_done, h * 2 + (k - 3))
                            e = (k - 4) * CW
                            V.tensor_tensor(v_lo[:, :, e:e + CW],
                                            ps[:, 2 * (k - 4):2 * (k - 4) + 2].rearrange("p b (t n) -> p (b t) n", t=2),
                                            raw_f32(v_hi[:, :, e:e + CW]), ALU.subtract).then_inc(v_lo_done, 1)
                    for I in range(TT):
                        E = h * TT + I
                        dve.wait_ge(pv_done, E + 1)
                        st(V.bn_stats(bn[:, 0, 0:6], ps[:, 5 + 2 * (I % 2)]))
                        st.wait()
                        dve.sem_inc(bn_ready, 1)
                        st(V.bn_aggr(bn[:, 1, 0:2], bn[:, 0, 0:6]))
                        st.wait()
                        V.tensor_scalar(gn[:, I % 2, 0:1], bn[:, 1, 1:2], GN_EPS, None, ALU.add).then_inc(gn_var, 1)
                        if I + 1 < TT:
                            scores_masked(h, I + 1)
                        dve.wait_ge(gn_rstd, E + 1)
                        dve.wait_ge(o_turned, E + 1)
                        V.tensor_scalar(o_n, ps[:, 5 + 2 * (I % 2)], bn[:, 1, 0:1], gn[:, I % 2, 1:2],
                                        ALU.subtract, ALU.mult).then_inc(o_normed, 1)
                        dve.wait_ge(o_turned, E + 2)
                        dve.wait_ge(sil_g_done, h * 2 + 2)
                        V.tensor_tensor(s_buf[:, 0].rearrange("p (t n) -> p t n", t=TT),
                                        ps[:, 6].rearrange("p (t n) -> p t n", t=TT),
                                        sil_g[:, :, I * P:(I + 1) * P], ALU.mult).then_inc(gated, 1)
                        dve.wait_ge(a_hi_done, E + 1)
                        a = (slice(None), bass.ds(h * TT, TT), slice(I * P, (I + 1) * P))
                        V.tensor_tensor(g_lo[a], s_buf[:, 0].rearrange("p (t n) -> p t n", t=TT),
                                        raw_f32(g_hi[a]), ALU.subtract).then_inc(a_lo_done, 1)

            def scores_masked(h, I):
                E = h * TT + I
                W = (I + 1) * P
                dve.wait_ge(score_done, E + 1)
                if I == 0:
                    dve.wait_ge(decay_in, h * 16 + 16)
                for J in range(I + 1):
                    c = (I - J) * P
                    ins = V.tensor_tensor(s_buf[:, 1, J * P:(J + 1) * P], ps[:, 4, J * P:(J + 1) * P],
                                          decay[:, c:c + P], ALU.mult)
                ins.then_inc(masked, 1)
                dve.wait_ge(s_hi_done, E + 1)
                V.tensor_tensor(s_lo[:, 0:W], s_buf[:, 1, 0:W], raw_f32(s_hi[:, 0:W]),
                                ALU.subtract).then_inc(s_lo_done, 1)

            def s5():
                S = small
                dve.wait_ge(hf_done, 5 * KT)
                dve.sem_inc(exp_in, 1)
                tt = lambda o, a, b, op: st(V.tensor_tensor(o, a, b, op))
                ts = lambda o, a, x, y, f, g: st(V.tensor_scalar(o, a, x, y, f, g))

                def w(*_):
                    st.wait()
                M, A_, Sb = ALU.mult, ALU.add, ALU.subtract
                dve.wait_ge(nat_turned, 1)
                st(V.tensor_copy(S["are"], ps[:, 7, 0:G]))
                st(V.tensor_copy(S["aim"], ps[:, 7, G:2 * G]))
                w()
                dve.sem_inc(a_copied, 1)
                dve.wait_ge(exp_done, 1)
                tt(S["x"], S["are"], S["dt"], M)
                tt(S["th"], S["aim"], S["dt"], M)
                w()
                ts(S["t1"], S["x"], float(SC), None, M, ALU.bypass)
                w()
                dve.sem_inc(exp_in, 1)
                reduce_turns(S["th"], S["cnt"])
                ts(S["half"], S["th"], 0.5, None, M, ALU.bypass)
                ts(S["arg"], S["th"], -0.5, None, M, ALU.bypass)
                w()
                tt(S["arg"], S["arg"], S["half"], ALU.min)
                w()
                ts(S["arg"], S["arg"], float(np.float32(np.pi / 2)), None, A_, ALU.bypass)
                w()
                dve.sem_inc(wave_in, 1)
                dve.wait_ge(wave_done, 1)
                ts(S["t2"], S["tn"], -1.0, 1.0, M, A_)
                w()
                st(V.reciprocal(S["t2"], S["t2"]))
                tt(S["s1"], S["sh"], S["ch"], M)
                tt(S["w"], S["sh"], S["sh"], M)
                w()
                st(V.scalar_tensor_tensor(out=S["em1"], in0=S["tn"], scalar=2.0, in1=S["t2"], op0=M, op1=M))
                ts(S["s1"], S["s1"], 2.0, None, M, ALU.bypass)
                ts(S["w"], S["w"], 2.0, None, M, ALU.bypass)
                w()
                ts(S["ex"], S["em1"], 1.0, None, A_, ALU.bypass)
                ts(S["c1"], S["w"], -1.0, 1.0, M, A_)
                w()
                tt(S["nre"], S["em1"], S["c1"], M)
                tt(S["nim"], S["ex"], S["s1"], M)
                w()
                tt(S["nre"], S["nre"], S["w"], Sb)
                tt(S["fre"], S["are"], S["are"], M)
                tt(S["fim"], S["aim"], S["aim"], M)
                w()
                tt(S["cnt"], S["fre"], S["fim"], A_)
                tt(S["t2"], S["nre"], S["are"], M)
                tt(S["half"], S["nim"], S["aim"], M)
                tt(S["arg"], S["nim"], S["are"], M)
                tt(S["tn"], S["nre"], S["aim"], M)
                w()
                st(V.reciprocal(S["cnt"], S["cnt"]))
                tt(S["t2"], S["t2"], S["half"], A_)
                tt(S["arg"], S["arg"], S["tn"], Sb)
                w()
                tt(S["fre"], S["t2"], S["cnt"], M)
                tt(S["fim"], S["arg"], S["cnt"], M)
                ts(S["a"], S["nre"], 1.0, None, A_, ALU.bypass)
                st(V.tensor_copy(S["b"], S["nim"]))
                st(V.memset(pw1[0:NS, :, 0], 1.0))
                st(V.memset(pw1[NS:P, :, 0], 0.0))
                st(V.memset(pw2[0:NS, :, 0], 0.0))
                st(V.memset(pw2[NS:P, :, 0], 1.0))
                w()
                for d in range(SC):
                    tt(S["x"], S["a"], pw1[:, :, d], M)
                    tt(S["t2"], S["b"], pw2[:, :, d], M)
                    tt(S["half"], S["a"], pw2[:, :, d], M)
                    tt(S["arg"], S["b"], pw1[:, :, d], M)
                    w()
                    tt(pw1[:, :, d + 1], S["x"], S["t2"], A_)
                    tt(pw2[:, :, d + 1], S["half"], S["arg"], Sb)
                    w()
                dve.wait_ge(nat_copied, 4)
                kb = lambda t: t.unsqueeze(2).broadcast_to([P, G, SK])
                sbb = s_buf[:].rearrange("p a (g k) -> p (a g) k", k=SK)
                tt(sbb, b_im[:], kb(S["fim"]), M)
                tt(bb_tmp[:], b_re[:], kb(S["fim"]), M)
                w()
                tt(b_re[:], b_re[:], kb(S["fre"]), M)
                tt(b_im[:], b_im[:], kb(S["fre"]), M)
                w()
                tt(b_re[:], b_re[:], sbb, Sb)
                tt(b_im[:], b_im[:], bb_tmp[:], A_)
                def square_turn():
                    tt(S["t2"], S["s1"], S["s1"], M)
                    tt(S["half"], S["s1"], S["c1"], M)
                    w()
                    ts(S["c1"], S["t2"], -2.0, 1.0, M, A_)
                    ts(S["s1"], S["half"], 2.0, None, M, ALU.bypass)
                    w()
                for _ in range(3):
                    square_turn()
                st(V.memset(ctab[:, :, 0:1], 1.0))
                st(V.memset(stab[:, :, 0:1], 0.0))
                w()
                n = 1
                while n < NC:
                    nb = lambda t: t.unsqueeze(2).broadcast_to([P, G, n])
                    lo, hi, tmp = slice(0, n), slice(n, 2 * n), tab_tmp[:, :, 0:n]
                    tt(ctab[:, :, hi], ctab[:, :, lo], nb(S["c1"]), M)
                    tt(tmp, stab[:, :, lo], nb(S["s1"]), M)
                    tt(stab[:, :, hi], stab[:, :, lo], nb(S["c1"]), M)
                    w()
                    tt(ctab[:, :, hi], ctab[:, :, hi], tmp, Sb)
                    w()
                    tt(tmp, ctab[:, :, lo], nb(S["s1"]), M)
                    w()
                    tt(stab[:, :, hi], stab[:, :, hi], tmp, A_)
                    w()
                    n *= 2
                    if n < NC:
                        square_turn()
                ts(stab[:], stab[:], sgn, None, M, ALU.bypass)
                w()
                dve.sem_inc(tabs_done, 1)
                dve.wait_ge(exp_done, 2)
                dve.wait_ge(zeroed, 3)
                v3 = lambda t: t.rearrange("p (g c) -> p g c", c=NC)
                yy, turned, rot, z = s_buf[:, 0], sq[:, 0], sq[:, 1], acc[:]
                dve.sem_inc(yd_done, 1)
                dve.sem_inc(a5_lo, 1)

                def output_powers(b, s):
                    if not (isinstance(b, int) and b < 2):
                        dve.wait_ge(y_done, b)
                    for half in range(2):
                        gs = bass.ds(b * GB + half * (GB // 2), GB // 2)
                        shape = [P, GB // 2, SC + 1, SK]
                        yh = ys[:, s, half * (GB // 2):(half + 1) * (GB // 2)]
                        if half:
                            w()
                        tt(yh, c_re[:, gs, :].unsqueeze(2).broadcast_to(shape),
                           pw1[:, gs, :].unsqueeze(3).broadcast_to(shape), M)
                        tt(yt[:], c_im[:, gs, :].unsqueeze(2).broadcast_to(shape),
                           pw2[:, gs, :].unsqueeze(3).broadcast_to(shape), M)
                        w()
                        tt(yh, yh, yt[:], A_)
                    w()
                    dve.sem_inc(ys_done, 1)

                def chunk_inputs(b, s):
                    dve.wait_ge(z_turned, b + 1)
                    V.tensor_copy(us[:, s].rearrange("p g c -> p (g c)"), ps[:, 2]).then_inc(us_done, 1)

                def odd_rows(b, s):
                    dve.wait_ge(m_early, b + 1)
                    for J in range(4):
                        q = slice(32 * J, 32 * J + 32)
                        wd = (2 * J + 1) * SK
                        ins = V.scalar_tensor_tensor(
                            out=mt[q, s, :, P - wd:P],
                            in0=ps[q, 5:7].rearrange("p a (g n) -> p (a g) n", n=P)[:, :, 0:wd],
                            scalar=even[q], in1=mt[q, s, :, P - wd:P], op0=M, op1=A_)
                    ins.then_inc(m_done, 1)

                def scan(b):
                    gs = bass.ds(b * GB, GB)
                    tt(v3(z), rho[:, gs].unsqueeze(2).broadcast_to([P, GB, NC]),
                       cmask.unsqueeze(1).broadcast_to([P, GB, NC]), M)
                    dve.wait_ge(v_done, b + 1)
                    tt(v3(turned)[0:NS], v3(ps[:, 7])[NS:P], stab[NS:P, gs, :], M)
                    tt(v3(turned)[NS:P], v3(ps[:, 7])[0:NS], stab[0:NS, gs, :], M)
                    tt(v3(rot), v3(ps[:, 7]), ctab[:, gs, :], M)
                    w()
                    tt(rot, rot, turned, Sb)
                    w()
                    st(V.tensor_tensor_scan(turned, z, rot, 0.0, M, A_))
                    w()
                    tt(v3(rot)[0:NS], v3(turned)[NS:P], stab[NS:P, gs, :], M)
                    tt(v3(rot)[NS:P], v3(turned)[0:NS], stab[0:NS, gs, :], M)
                    tt(v3(z), v3(turned), ctab[:, gs, :], M)
                    w()
                    if not (isinstance(b, int) and b == 0):
                        dve.wait_ge(y_done, b + 1)
                    tt(s_prev[:, :, 1:NC], v3(z)[:, :, 0:NC - 1], v3(rot)[:, :, 0:NC - 1], A_)
                    w()
                    dve.sem_inc(sp_done, 1)

                def skip(b):
                    dve.wait_ge(a5_lo, b + 1)
                    dve.wait_ge(yz_turned, b + 2)
                    V.scalar_tensor_tensor(out=yy.rearrange("p (c i) -> p c i", i=SC),
                                           in0=u[:, bass.ds(b, 1), :].rearrange("p a (c i) -> p (a c) i", i=SC),
                                           scalar=par[:, bass.ds(b + COL_D, 1)],
                                           in1=ps[:, 2].rearrange("p (i c) -> p c i", i=SC),
                                           op0=M, op1=A_).then_inc(yd_done, 1)

                def output_lo(b):
                    dve.wait_ge(a5_hi, b + 1)
                    V.tensor_tensor(h_lo[:, bass.ds(b, 1), :].rearrange("p a n -> p (a n)"), yy,
                                    raw_f32(h_hi[:, bass.ds(b, 1), :]).rearrange("p a n -> p (a n)"),
                                    Sb).then_inc(a5_lo, 1)

                output_powers(0, 0)
                chunk_inputs(0, 0)
                odd_rows(0, 0)
                scan(0)
                output_powers(1, 1)
                with st.loop(KT // 2 - 1, 32) as i:
                    for s in range(2):
                        b = i * 2 + s
                        chunk_inputs(i * 2 + (s + 1), 1 - s)
                        odd_rows(i * 2 + (s + 1), 1 - s)
                        scan(i * 2 + (s + 1))
                        skip(b)
                        output_powers(i * 2 + (s + 2), s)
                        output_lo(b)
                chunk_inputs(KT - 1, 1)
                odd_rows(KT - 1, 1)
                scan(KT - 1)
                skip(KT - 2)
                output_lo(KT - 2)
                skip(KT - 1)
                output_lo(KT - 1)
                w()
                st(V.memset(acc[:], 0.0))
                set_coef(1, 1, 1.0, 36)
                with st.loop(OUT_PAIRS, 4) as dp:
                    n = dp * 2 + C_GLU
                    split_lo(n + 1, 1)
                    split_lo(n + 2, 0)
                    dve.wait_ge(w_used, n + 3)
                    dve.wait_ge(gate_done, dp + 1)
                    tt(s_buf[:], s_buf[:], ps[:, 2:4], M)
                    w()
                    for t in range(2):
                        tile = bass.ds(dp * 2 + t, 1)
                        ins_ = V.scalar_tensor_tensor(out=x_sb[:, tile, :], in0=s_buf[:, t:t + 1, :],
                                                      scalar=coef[:, tile], in1=x_sb[:, tile, :], op0=M, op1=A_)
                    st(ins_)
                    w()
                    dve.sem_inc(x_done, 1)
                    add_squares(dp + 5 * OUT_PAIRS)

            for s in (w_lo_done, ada_used, ada_used, x_done, acc_done, xn_done, prod_done,
                      g_lo_done, masked, a_lo_done, v_lo_done, rot_lo_done):
                dve.sem_inc(s, 1)
            st(V.memset(acc[:], 0.0))
            dve.wait_ge(rows_turned, 1)
            V.tensor_copy(par[:], ps[:, 7, 0:3 * 72]).then_inc(par_done, 1)
            for pr in range(OUT_PAIRS):
                add_squares(pr)
                dve.sem_inc(x_done, 1)
            dve.wait_ge(csil_done, 1)
            for q in range(ADA_FIRST):
                dve.wait_ge(ada0_in[q], 32)
                if q:
                    dve.wait_ge(ada_summed, q)
                ada_terms(ada_first[:, q], 0, ada_acc[:], True)
                st.wait()
                dve.sem_inc(ada_acc_done, 1)
                dve.wait_ge(ada_summed, q + 1)
                V.tensor_tensor(mods[:, 4 * q:4 * q + 4], ps[:, 6, 0:4], par[:, 4 * q:4 * q + 4],
                                ALU.add).then_inc(mods_done, 1)
            dve.wait_ge(w_hi_done, 2)
            V.tensor_tensor(w_lo[0][:], w_raw[0][:], raw_f32(w_hi[0][:]), ALU.subtract).then_inc(w_lo_done, 1)
            norm(0, 0, 0)
            ffn(0)
            norm(1, 0, 1)
            retention()
            set_coef(0, 1, 1.0, 18)
            dve.wait_ge(back_done, 16)
            out_phase(C_RET_OUT, RET_OUT, OUT_PAIRS * 2)
            norm(2, 0, 2)
            ffn(1)
            norm(3, 1, 0)
            ffn(2)
            norm(4, 1, 1, "u")
            s5()
            norm(5, 1, 2)
            ffn(3, True)
            norm(6, 0, 0, "out")

        @block.tensor
        def _(pe):
            def mm3(o, wh, wl, xh, xl, start, stop):
                nc.tensor.matmul(o, wl, xh, start=start, stop=False)
                nc.tensor.matmul(o, wh, xl, start=False, stop=False)
                return nc.tensor.matmul(o, wh, xh, start=False, stop=stop)

            def chunk(n, k, xh, xl, r0, r, bank, first, last, h_from=None):
                pe.wait_ge(w_lo_done, n + 2)
                s = k % 2
                for t in range(r):
                    if h_from is not None:
                        pe.wait_ge(h_lo_done, h_from + t + 1)
                    for c in range(2):
                        m = mm3(ps[:, bank + c], w_hi[s][:, t, c * P:(c + 1) * P], w_lo[s][:, t, c * P:(c + 1) * P],
                                xh[:, r0 + t], xl[:, r0 + t], first and t == 0, last and t == r - 1)
                m.then_inc(w_used, 1)

            def ada_sum(Q):
                pe.wait_ge(ada_acc_done, Q + (ADA_FIRST + 1))
                pe.wait_ge(mods_done, Q + ADA_FIRST)
                for c in range(4):
                    m = nc.tensor.matmul(ps[:, 6, c:c + 1], ada_acc[:, c * P:(c + 1) * P], ones[:, 0:1],
                                         start=True, stop=True)
                m.then_inc(ada_summed, 1)

            def norm(k, kind="h"):
                pe.wait_ge(acc_done, OUT_PAIRS * (k + 1) + 1)
                for t in range(TT):
                    m = nc.tensor.matmul(ps[:, 4, t:t + 1], acc[:, t * P:(t + 1) * P], ones[:, 0:1],
                                         start=True, stop=True)
                m.then_inc(stat_done, 1)
                pe.wait_ge(diag_done, k + 1)
                nc.tensor.matmul(ps[:, 5], ones[:], sq[:, 0], start=True, stop=True).then_inc(rbc_done, 1)
                if kind == "out":
                    for t in range(KT):
                        pe.wait_ge(hf_done, KT * k + t + 1)
                        if t >= 2:
                            pe.wait_ge(y_copied, t - 1)
                        for j in range(TT):
                            m = nc.tensor.transpose(ps[:, t % 2, j * P:(j + 1) * P],
                                                    slots[t % 4][:, j * P:(j + 1) * P], ident[:])
                        m.then_inc(y_turned, 1)

            def out_phase(n0, chunks, pair0, xh, xl, ada=None):
                m = len(chunks)
                with pe.Fori(0, 2) as j:
                    n = j * (2 * m) + n0
                    for dp in range(2):
                        pe.wait_ge(x_done, j * 2 + (pair0 + dp))
                        for c, r in enumerate(chunks):
                            k = dp * m + c
                            chunk(n + k, k, xh, xl, 8 * c, r, 2 * dp, c == 0, c == m - 1)
                        if ada is not None:
                            ada_sum(j * 2 + (ada + dp))

            def ffn(f):
                n0 = C_FFN[f]
                a_in, a_out = ADA_AT[f]
                hk = HK[NORM_OF[f]] * KT
                def in_pair(i, ada):
                    pe.wait_ge(silu_done, i + (FFN_PAIRS * f + 1))
                    chunk(i * 2 + n0, 0, h_hi, h_lo, 0, 8, 0, True, True, h_from=hk)
                    pe.wait_ge(prod_done, i + (FFN_PAIRS * f + 1))
                    chunk(i * 2 + (n0 + 1), 1, h_hi, h_lo, 0, 8, 2, True, True)
                    if ada:
                        ada_sum(i + a_in)
                with pe.Fori(0, ADA_IN) as i:
                    in_pair(i, a_in is not None)
                in_pair(ADA_IN, False)
                pe.wait_ge(g_lo_done, FFN_PAIRS * (f + 1) + 1)
                out_phase(n0 + 2 * FFN_PAIRS, FFN_OUT, OUT_PAIRS * (SUB[f] + 1), g_hi, g_lo, a_out)

            def retention():
                hk = HK[1] * KT
                with pe.Fori(0, HEADS) as h:
                    n = h * 6 + C_RET
                    for k in range(4):
                        if k == 0:
                            pe.wait_ge(v_lo_done, h * 2 + 1)
                        elif k == 2:
                            pe.wait_ge(a_lo_done, h * TT + 1)
                        chunk(n + k, k, h_hi, h_lo, 0, 8, 2 * k, True, True, h_from=hk if k == 0 else None)
                    pe.wait_ge(rot_lo_done, h * 2 + 3)
                    for k in (4, 5):
                        pe.wait_ge(w_lo_done, n + (k + 2))
                        s = k % 2
                        for t in range(TT):
                            o = ps[:, 2 * (k - 4) + t // 2, (t % 2) * CW:(t % 2 + 1) * CW]
                            for r in range(KT):
                                at = slice(t * P, (t + 1) * P)
                                m = mm3(o, h_hi[:, r, at], h_lo[:, r, at], w_hi[s][:, r, :], w_lo[s][:, r, :],
                                        r == 0, r == KT - 1)
                        m.then_inc(w_used, 1)
                        if k == 4:
                            scores(h, 0)
                    pe.wait_ge(v_lo_done, h * 2 + 3)
                    for I in range(TT):
                        E = h * TT + I
                        pe.wait_ge(s_lo_done, E + 1)
                        for J in range(I + 1):
                            at = slice(J * P, (J + 1) * P)
                            m = mm3(ps[:, 5 + 2 * (I % 2)], s_hi[:, at], s_lo[:, at], v_hi[:, J], v_lo[:, J],
                                    J == 0, J == I)
                        m.then_inc(pv_done, 1)
                        if I + 1 < TT:
                            scores(h, I + 1)
                        pe.wait_ge(o_normed, E + 1)
                        for t in range(TT):
                            m = nc.tensor.transpose(ps[:, 6, t * P:(t + 1) * P], o_n[:, t * P:(t + 1) * P], ident[:])
                        m.then_inc(o_turned, 1)

            def scores(h, I):
                pe.wait_ge(sil_g_done, h * 2 + 2)
                Q = slice(I * P, (I + 1) * P)
                for J in range(I + 1):
                    K = slice(J * P, (J + 1) * P)
                    for t in range(2):
                        m = mm3(ps[:, 4, K], k_hi[:, t, K], k_lo[:, t, K], q_hi[:, t, Q], q_lo[:, t, Q], t == 0, t == 1)
                m.then_inc(score_done, 1)

            def s5():
                T_ = nc.tensor.transpose
                pe.wait_ge(nat_in, 16 * 10)
                for r in range(2):
                    m = T_(ps[:, 7, r * G:(r + 1) * G], a_nat[:, r], ident[0:NS, 0:NS])
                m.then_inc(nat_turned, 1)
                for r in range(2):
                    bk = b_nat[:, r].rearrange("g (p k) -> g k p", k=SK)
                    for k in range(SK):
                        m = T_(ps[0:NS, 2 * r + k // 8, (k % 8) * G:(k % 8 + 1) * G],
                               bk[:, k, :], ident[0:NS, 0:NS])
                    m.then_inc(nat_turned, 1)
                pe.wait_ge(xn_done, 1 + 5 * KT)
                pe.wait_ge(a_copied, 1)
                for r in range(2):
                    if r:
                        pe.wait_ge(exp_in, 2)
                    for t in range(KT):
                        m = T_(ps[:, 4 + 2 * r + t // 4, (t % 4) * P:(t % 4 + 1) * P], c_nat[:, r, t], ident[:])
                    m.then_inc(nat_turned, 1)
                pe.wait_ge(nat_copied, 4)
                for s in (y_done, yz_turned):
                    pe.sem_inc(s, 1)

                def front(b, s, first=False):
                    pe.wait_ge(ub_done, b + 1)
                    if not first:
                        pe.wait_ge(yz_done, b)
                    pe.sem_inc(pe_passed, 1)
                    ub = s_buf[:, 1].rearrange("p (c j) -> p j c", j=SC)
                    for j in range(SC):
                        m = T_(ps[0:NC, j // 4, (j % 4) * P:(j % 4 + 1) * P], ub[:, SC - 1 - j, :], ident[:])
                    m.then_inc(u_turned, 1)
                    pe.wait_ge(xs_done, b + 1)
                    if not first:
                        pe.wait_ge(win_done, b)
                    pe.sem_inc(pe_passed, 1)
                    for g in range(GB):
                        m = T_(ps[:, 3 + g // 4, (g % 4) * P:(g % 4 + 1) * P],
                               xs[:, g].rearrange("p j k -> p (j k)"), ident[:])
                    m.then_inc(xs_turned, 1)
                    pe.wait_ge(ys_done, b + 1)
                    pe.wait_ge(rows_done, b + 1)
                    if not first:
                        pe.wait_ge(m_done, b)
                    for g in range(GB):
                        m = nc.tensor.matmul(ps[:, 5 + g // 4, (g % 4) * P:(g % 4 + 1) * P], b_rows[:, g],
                                             ys[:, s, g, 0:SC, :].rearrange("p d k -> p (d k)"),
                                             start=True, stop=True)
                    m.then_inc(lag_done, 1)
                    pe.wait_ge(z_done, b + 1)
                    if not first:
                        pe.wait_ge(yd_done, b)
                    pe.sem_inc(pe_passed, 1)
                    for g in range(GB):
                        m = T_(ps[:, 2, g * NC:(g + 1) * NC], zt[:, g * P:(g + 1) * P], ident[0:NC, 0:NC])
                    m.then_inc(z_turned, 1)

                def states(b, s):
                    pe.wait_ge(win_done, b + 1)
                    pe.wait_ge(us_done, b + 1)
                    if not (isinstance(b, int) and b == 0):
                        pe.wait_ge(sp_done, b)
                    for g in range(GB):
                        m = nc.tensor.matmul(ps[:, 7, g * NC:(g + 1) * NC], win[:, g], us[:, s, g],
                                             start=True, stop=True)
                    m.then_inc(v_done, 1)

                def outputs(b, s):
                    pe.wait_ge(m_done, b + 1)
                    pe.wait_ge(sp_done, b + 1)
                    for g in range(GB):
                        o = ps[0:NC, g // 4, (g % 4) * P:(g % 4 + 1) * P]
                        nc.tensor.matmul(o, us[:, s, g], mt[:, s, g], start=True, stop=False)
                        m = nc.tensor.matmul(o, s_prev[:, g], ys[:, s, g, 1:SC + 1, :].rearrange("p d k -> p (d k)"),
                                             start=False, stop=True)
                    m.then_inc(y_done, 1)

                def turn_back(b):
                    pe.wait_ge(yz_done, b + 2)
                    pe.sem_inc(pe_passed, 1)
                    for i in range(SC):
                        m = T_(ps[:, 2, i * NC:(i + 1) * NC], zt[:, i * P:(i + 1) * P], ident[0:NC, 0:NC])
                    m.then_inc(yz_turned, 1)

                front(0, 0, True)
                states(0, 0)
                with pe.Fori(0, KT // 2 - 1) as i:
                    for s in range(2):
                        front(i * 2 + (s + 1), 1 - s)
                        states(i * 2 + (s + 1), 1 - s)
                        outputs(i * 2 + s, s)
                        turn_back(i * 2 + s)
                front(KT - 1, 1)
                states(KT - 1, 1)
                outputs(KT - 2, 0)
                turn_back(KT - 2)
                outputs(KT - 1, 1)
                turn_back(KT - 1)
                pe.wait_ge(a5_lo, KT + 1)
                pe.wait_ge(m_early, KT)
                with pe.Fori(0, OUT_PAIRS) as dp:
                    n = dp * 2 + C_GLU
                    pe.wait_ge(x_done, dp + (5 * OUT_PAIRS + 1))
                    chunk(n, 0, h_hi, h_lo, 0, 8, 0, True, True)
                    chunk(n + 1, 1, h_hi, h_lo, 0, 8, 2, True, True)

            for s in (w_used, o_turned):
                pe.sem_inc(s, 1)
            pe.wait_ge(consts, 4)
            pe.wait_ge(rows_in, 16 * 7)
            for r in range(3):
                m = nc.tensor.transpose(ps[:, 7, 72 * r:72 * r + 72], sq[0:72, 0, r * P:(r + 1) * P],
                                        ident[0:72, 0:72])
            m.then_inc(rows_turned, 1)
            for t in range(TT):
                pe.wait_ge(x_in[t], 16)
            for k in range(KT):
                if k >= 4 and k % 2 == 0:
                    pe.wait_ge(x_copied, (k - 4) // 2 + 1)
                for t in range(TT):
                    m = nc.tensor.transpose(ps[:, k % 4, t * P:(t + 1) * P], x_tok[:, t, k * P:(k + 1) * P], ident[:])
                m.then_inc(x_turned, 1)
            for q in range(ADA_FIRST):
                pe.wait_ge(ada_acc_done, q + 1)
                if q:
                    pe.wait_ge(mods_done, q)
                for c in range(4):
                    m = nc.tensor.matmul(ps[:, 6, c:c + 1], ada_acc[:, c * P:(c + 1) * P], ones[:, 0:1],
                                         start=True, stop=True)
                m.then_inc(ada_summed, 1)
            norm(0)
            ffn(0)
            norm(1)
            retention()
            pe.wait_ge(a_lo_done, 1 + HEADS * TT)
            out_phase(C_RET_OUT, RET_OUT, OUT_PAIRS * 2, g_hi, g_lo)
            norm(2)
            ffn(1)
            norm(3)
            ffn(2)
            norm(4)
            s5()
            norm(5)
            ffn(3)
            norm(6, "out")


NORM_OF = {0: 0, 1: 2, 2: 3, 3: 5}
SUB = {0: 0, 1: 2, 2: 3, 3: 5}
HK = {0: 0, 1: 1, 2: 2, 3: 3, 5: 4}
MODS_NEED = {0: 4, 1: 18, 2: 18, 3: 32, 4: 36, 5: 36}


def landed(n, k):
    return (n - k % 2) * 8 + 16


_INS = ["x", "c", "positions", "ada_w", "ada_b", "norm_g", "ffn_w_in", "ffn_w_out", "ret_w_in", "ret_w_out",
        "s5_a_re", "s5_a_im", "s5_b_re", "s5_b_im", "s5_c_re", "s5_c_im", "s5_d", "s5_log_dt", "s5_w_glu", "final_g"]


def shape_constants():
    half = D // HEADS // 2
    inv_freq = (np.float32(10000.0) ** (-np.arange(half, dtype=np.float32) / np.float32(half))).astype(np.float32)
    log_gamma = np.log(1.0 - 2.0 ** (-5.0 - np.arange(HEADS)))
    c, j = np.arange(L)[None, None, :], np.arange(P)[None, :, None]
    decay = np.where(c >= j, np.exp(log_gamma[:, None, None] * np.maximum(c - j, 0)), 0.0)
    p = np.arange(P)
    s5_const = np.concatenate([np.where(p < NS, 1.0, -1.0)[:, None], (p // SK % 2 == 0)[:, None],
                               (p // SK % 2 == 1)[:, None], np.repeat(np.arange(NC)[None] > 0, P, 0)], 1)
    return {"s5_const": s5_const.astype(np.float32), "inv_freq": inv_freq[:, None],
            "decay": (decay / np.sqrt(D // HEADS)).astype(np.float32)}


def kernel(**inputs):
    import numpy as _np
    import concourse.bacc as _bacc
    from concourse.bass_utils import run_bass_kernel_spmd as _run

    nc = _bacc.Bacc("TRN2", target_bir_lowering=False, num_devices=1)
    arrays, ins = {}, {}
    for name, a in [(n, inputs[n]) for n in _INS] + list(shape_constants().items()):
        a = _np.ascontiguousarray(a)
        arrays[f"in_{name}"] = a
        ins[name] = nc.dram_tensor(f"in_{name}", a.shape, mybir.dt.from_np(a.dtype), kind="ExternalInput").ap()
    out = nc.dram_tensor("out_y", (1, L, D), F32, kind="ExternalOutput").ap()
    build(nc, ins, out)
    r = _run(nc, [arrays], core_ids=[0])
    return r.results[0]["out_y"]
```

```python
from contextlib import ExitStack, contextmanager

import numpy as np

import concourse.bass as bass
from concourse import mybir

F32 = mybir.dt.float32
F32R = mybir.dt.float32r
I32 = mybir.dt.int32
ALU = mybir.AluOpType
ACT = mybir.ActivationFunctionType

P = 128
D = 1024
L = 512
KT = D // P
TT = L // P
FF = 2816
FT = FF // P
N_MOD = 9
HEADS = 4
DV = 2 * D // HEADS
CW = 256
NORM_EPS = 1e-6
GN_EPS = 1e-5

FFN_PAIRS = FT // 2
FFN_OUT = (8, 8, 6)
RET_OUT = (8, 8)
OUT_PAIRS = KT // 2

C_FFN = [0, 66, 100, 142]
C_RET = 34
C_RET_OUT = C_RET + 6 * HEADS
C_GLU = 134
N_CHUNKS = 176

ADA_W = 512
ADA_FIRST = 4
ADA_IN = FFN_PAIRS - 1
ADA_AT = {0: (0, 10), 1: (14, 24), 2: (None, 28), 3: (None, None)}

G, NS, SK = 64, 64, 16
SC = P // SK
NC = L // SC
GB = P // SK
S5_LEFT = {"ctab": ([P, G, NC], F32), "stab": ([P, G, NC], F32),
           "b_re": ([P, G, SK], F32), "b_im": ([P, G, SK], F32), "c_re": ([P, G, SK], F32),
           "c_im": ([P, G, SK], F32), "pw1": ([P, G, SC + 1], F32), "pw2": ([P, G, SC + 1], F32)}
S5_LOAD = {"b_nat": ([NS, 2, NS * SK], F32), "c_nat": ([P, 2, KT, P], F32), "a_nat": ([NS, 2, P], F32)}
S5_TABLE = {"tab_tmp": ([P, G, NC // 2], F32), "bb_tmp": ([P, G, SK], F32)}
S5_WORK = {"xs": ([P, GB, SC, SK], F32), "xt": ([P, GB // 2, SC, SK], F32),
           "ys": ([P, 2, GB, SC + 1, SK], F32), "yt": ([P, GB // 2, SC + 1, SK], F32),
           "zt": ([NS, GB * P], F32), "sp": ([P, GB, NC], F32), "b_rows": ([P, GB, P], F32),
           "mt": ([P, 2, GB, P], F32)}
S5_RIGHT = {"x_again": ([P, KT, L], F32), "win": ([P, GB, P], F32), "us": ([P, 2, GB, NC], F32)}
SMALL = ("are aim x th cnt half arg sh ch tn em1 ex w s1 c1 nre nim a b fre fim t1 t2").split()

COL_G = 2 * N_MOD * KT
COL_FG = COL_G + 6 * KT
COL_D = COL_FG + KT
COL_C = COL_D + KT


class Steps:

    def __init__(self, eng, sem):
        self.eng, self.sem, self.n, self.i, self.per = eng, sem, 0, None, 0

    def value(self):
        return self.n if self.i is None else self.i * self.per + self.n

    def __call__(self, ins):
        ins.then_inc(self.sem, 1)
        self.n += 1
        return ins

    def wait(self):
        self.eng.wait_ge(self.sem, self.value())

    @contextmanager
    def loop(self, count, per):
        with self.eng.Fori(0, count) as i:
            start = self.n
            self.i, self.per = i, per
            yield i
            assert self.n - start == per, (self.n - start, per)
            self.i = None
            self.n = start + per * count


def build(nc, ins, out):
    x_d, c_d, pos_d = ins["x"], ins["c"], ins["positions"]
    ctx = ExitStack()
    with ctx:
        def sb(name, shape, dt=F32, **k):
            return ctx.enter_context(nc.sbuf_tensor(name, shape, dt, **k))

        def sem(name):
            return ctx.enter_context(nc.semaphore(name))

        h_hi = sb("h_hi", [P, KT, L], F32R)
        with ExitStack() as shared:
            h_lo = shared.enter_context(nc.sbuf_tensor("h_lo", [P, KT, L], F32R))
        u = sb("u", [P, KT, L])
        w_raw = [sb(f"w_raw{s}", [P, 8, CW]) for s in range(2)]
        w_hi = [sb(f"w_hi{s}", [P, 8, CW], F32R) for s in range(2)]
        w_lo = [sb(f"w_lo{s}", [P, 8, CW], F32R) for s in range(2)]
        s_buf = sb("s_buf", [P, 2, L])
        sq = sb("sq", [P, 2, L])
        acc = sb("acc", [P, L])
        ident = sb("ident", [P, P])
        ones = sb("ones", [P, P])
        mods = sb("mods", [P, 2 * N_MOD * KT])
        par = sb("par", [P, 3 * N_MOD * KT])
        csil = sb("csil", [P, KT])
        scale1 = sb("scale1", [P, KT])
        coef = sb("coef", [P, KT])
        ms = sb("ms", [P, TT])
        rstd = sb("rstd", [P, TT])
        mhalf = sb("mhalf", [P, TT])
        bn = sb("bn", [P, 2, 8])
        gn = sb("gn", [P, 2, 2])
        freq = sb("freq", [P, 1])

        def zone(side, *sets):
            for tensors in sets:
                with ExitStack() as z:
                    for name, (shape, dt) in tensors.items():
                        again = name in T
                        t = z.enter_context(nc.sbuf_tensor(name + f"_{len(T)}" * again, shape, dt, side=side))
                        T.setdefault(name, t)

        T = {}
        zone("left",
             {"g_hi": ([P, FT, L], F32R), "g_lo": ([P, FT, L], F32R)},
             {"x_tok": ([P, TT, D], F32), "ada_first": ([P, ADA_FIRST, KT, ADA_W], F32)},
             {**S5_LEFT, **S5_LOAD}, {**S5_LEFT, **S5_TABLE}, {**S5_LEFT, **S5_WORK})
        hold = ctx.enter_context(nc.sbuf_tensor("hold", [P, 2 * FT * L], F32))
        zone("right",
             {"x_sb": ([P, KT, L], F32), "ada_raw": ([P, 2, 2, ADA_W], F32), "ada_acc": ([P, ADA_W], F32)},
             {"k_hi": ([P, 2, L], F32R), "k_lo": ([P, 2, L], F32R), "o_t": ([P, TT, L], F32),
              "s_hi": ([P, L], F32R), "s_lo": ([P, L], F32R),
              "cos": ([P, L], F32), "sin": ([P, L], F32), "decay": ([P, L], F32)},
             S5_RIGHT)
        g_hi, g_lo, x_tok, ada_first = T["g_hi"], T["g_lo"], T["x_tok"], T["ada_first"]
        x_sb, ada_raw, ada_acc = T["x_sb"], T["ada_raw"], T["ada_acc"]
        k_hi, k_lo, o_t, s_hi, s_lo = T["k_hi"], T["k_lo"], T["o_t"], T["s_hi"], T["s_lo"]
        cos, sin, decay = T["cos"], T["sin"], T["decay"]
        o_n = sq[:, 0, :]
        RT = HEADS * DV // P
        v_hi, v_lo = g_hi[:, RT:RT + TT, :], g_lo[:, RT:RT + TT, :]
        q_hi, q_lo = g_hi[:, RT + TT:RT + TT + 2, :], g_lo[:, RT + TT:RT + TT + 2, :]
        slots = [s_buf[:, 0], s_buf[:, 1], sq[:, 0], sq[:, 1]]
        x_spill = nc.dram_tensor("x_spill", [P, KT, L], F32, kind="Internal").ap()

        ps = ctx.enter_context(nc.psum_tensor("ps", [P, 8, L], F32))

        w_landed = [sem(f"w_landed{s}") for s in range(2)]
        w_hi_done, w_lo_done, w_used = sem("w_hi_done"), sem("w_lo_done"), sem("w_used")
        consts, rows_in, x_in = sem("consts"), sem("rows_in"), [sem(f"x_in{t}") for t in range(TT)]
        ada0_in = [sem(f"ada0_in{q}") for q in range(ADA_FIRST)]
        rows_turned, par_done, csil_done = sem("rows_turned"), sem("par_done"), sem("csil_done")
        x_turned, x_copied = sem("x_turned"), sem("x_copied")
        ada_landed = [sem(f"ada_landed{s}") for s in range(2)]
        ada_used, ada_acc_done, ada_summed, mods_done = (
            sem("ada_used"), sem("ada_acc_done"), sem("ada_summed"), sem("mods_done"))
        x_done, sq_done, acc_done, stat_done = sem("x_done"), sem("sq_done"), sem("acc_done"), sem("stat_done")
        ms_done, rstd_done, rbc_done = sem("ms_done"), sem("rstd_done"), sem("rbc_done")
        xn_done, hf_done, h_hi_done, h_lo_done = sem("xn_done"), sem("hf_done"), sem("h_hi_done"), sem("h_lo_done")
        silu_done, prod_done, g_hi_done, g_lo_done = (
            sem("silu_done"), sem("prod_done"), sem("g_hi_done"), sem("g_lo_done"))
        spill_done, back_done = sem("spill_done"), sem("back_done")
        y_turned, y_copied, stored = sem("y_turned"), sem("y_copied"), sem("stored")
        dve_steps, act_steps = sem("dve_steps"), sem("act_steps")
        ang_done, trig_done, rot_in = sem("ang_done"), sem("trig_done"), sem("rot_in")
        rot_done, rot_hi_done, rot_lo_done = sem("rot_done"), sem("rot_hi_done"), sem("rot_lo_done")
        silu_g_done = sem("silu_g_done")
        v_hi_done, v_lo_done = sem("v_hi_done"), sem("v_lo_done")
        score_done, masked, s_hi_done, s_lo_done = sem("score_done"), sem("masked"), sem("s_hi_done"), sem("s_lo_done")
        pv_done, gn_var, gn_rstd, o_normed = sem("pv_done"), sem("gn_var"), sem("gn_rstd"), sem("o_normed")
        o_turned, gated, a_hi_done, a_lo_done = sem("o_turned"), sem("gated"), sem("a_hi_done"), sem("a_lo_done")
        decay_in, bn_ready, o_t_done = sem("decay_in"), sem("bn_ready"), sem("o_t_done")

        s5_const = sb("s5_const", [P, 3 + NC])
        sgn, even, odd, cmask = s5_const[:, 0:1], s5_const[:, 1:2], s5_const[:, 2:3], s5_const[:, 3:3 + NC]
        rho, dt = sb("rho", [P, G]), sb("dt", [P, G])
        small = {n: (sq if r < 16 else acc)[:].rearrange("p a n -> p (a n)" if r < 16 else "p n -> p n")[
                     :, (r % 16) * G:(r % 16 + 1) * G] for r, n in enumerate(SMALL)}
        ctab, stab, pw1, pw2 = T["ctab"], T["stab"], T["pw1"], T["pw2"]
        b_re, b_im, c_re, c_im = T["b_re"], T["b_im"], T["c_re"], T["c_im"]
        b_nat, c_nat, a_nat = T["b_nat"], T["c_nat"], T["a_nat"]
        tab_tmp, bb_tmp = T["tab_tmp"], T["bb_tmp"]
        xs, xt, ys, yt, zt, s_prev = T["xs"], T["xt"], T["ys"], T["yt"], T["zt"], T["sp"]
        win, mt, us = T["win"], T["mt"], T["us"]
        b_rows = T["b_rows"]
        nat_in, dt_in, nat_turned = sem("nat_in"), sem("dt_in"), sem("nat_turned")
        bank7_read = sem("bank7_read")
        a_copied, nat_copied = sem("a_copied"), sem("nat_copied")
        exp_done, wave_in, wave_done = sem("exp_done"), sem("wave_in"), sem("wave_done")
        tabs_done, zeroed, pool_steps = sem("tabs_done"), sem("zeroed"), sem("pool_steps")
        turn_done, tabs_half, consts_e = sem("turn_done"), sem("tabs_half"), sem("consts_e")
        (ub_done, u_turned, z_done, z_turned, us_done, xs_step, xs_done, xs_turned, win_done, ys_done, lag_done,
         m_early, m_done, v_done, sp_done, y_done, yz_done, yz_turned, yd_done, gelu_done, a5_hi, a5_lo, gate_done, rows_done, pe_passed
         ) = (sem("s5_" + n) for n in (
             "ub u_turned z z_turned us xs_step xs xs_turned win ys lag m_early m v sp y yz yz_turned yd gelu "
             "hi lo gate b_rows pe_passed").split())

        def raw_f32(ap):
            return ap.bitcast(F32)

        def rows(w):
            return w.rearrange("(t p) n -> p t n", p=P)

        ffn_in = [rows(ins["ffn_w_in"][f // 2, f % 2]) for f in range(4)]
        ffn_out = [rows(ins["ffn_w_out"][f // 2, f % 2]) for f in range(4)]
        ret_in, ret_out = rows(ins["ret_w_in"][0]), rows(ins["ret_w_out"][0])
        glu_w = rows(ins["s5_w_glu"][0])
        ada_w = [rows(ins["ada_w"][l]) for l in range(2)]

        block = ctx.enter_context(nc.Block())

        @block.sync
        def _(sp):
            def load(n, k, src, first=False):
                if not first:
                    sp.wait_ge(w_lo_done, n)
                sp.dma_start(w_raw[k % 2][:, 0:src.shape[1], :], src).then_inc(w_landed[k % 2], 16)

            def load_ada(Q, l, q):
                for p in range(4):
                    sp.wait_ge(ada_used, Q * 4 + (p + 1))
                    src = ada_w[l][:, 2 * p:2 * p + 2, bass.ds(q * ADA_W, ADA_W)]
                    sp.dma_start(ada_raw[:, p % 2], src).then_inc(ada_landed[p % 2], 16)

            def ffn(f):
                n0 = C_FFN[f]
                a_in, a_out = ADA_AT[f]
                def q_of(Q):
                    return (0, Q + ADA_FIRST) if f == 0 else (1, Q - 14)

                def in_pair(i, n, first, ada):
                    load(n, 0, ffn_in[f][:, :, bass.ds(i * CW, CW)], first)
                    load(n + 1, 1, ffn_in[f][:, :, bass.ds(i * CW + FF, CW)], first)
                    if ada:
                        load_ada(i + a_in, *q_of(i + a_in))
                if f == 0:
                    in_pair(0, 0, True, True)
                with sp.Fori(1 if f == 0 else 0, ADA_IN) as i:
                    in_pair(i, i * 2 + n0, False, a_in is not None)
                in_pair(ADA_IN, n0 + 2 * ADA_IN, False, False)
                with sp.Fori(0, 2) as j:
                    n, k = j * 6 + (n0 + 2 * FFN_PAIRS), 0
                    for dp in range(2):
                        for c, r in enumerate(FFN_OUT):
                            load(n + k, k, ffn_out[f][:, 8 * c:8 * c + r, bass.ds(j * 2 * CW + dp * CW, CW)])
                            k += 1
                        if a_out is not None:
                            Q = j * 2 + (a_out + dp)
                            load_ada(Q, *q_of(Q))

            def retention():
                def head_chunk(h, k):
                    at = (h * CW, h * CW + D, h * DV + 2 * D, h * DV + (2 * D + CW),
                          h * DV + 4 * D, h * DV + (4 * D + CW))[k]
                    load(h * 6 + (C_RET + k), k, ret_in[:, :, bass.ds(at, CW)])

                def out_chunk(dp, k):
                    m = len(RET_OUT)
                    c = k % m
                    load(dp * m + C_RET_OUT + c, c, ret_out[:, 8 * c:8 * c + 8, bass.ds(dp * CW, CW)])

                def head(h):
                    head_chunk(h, 2)
                    head_chunk(h, 3)
                    sp.wait_ge(masked, h * TT + 1)
                    sp.dma_start(decay[:], ins["decay"][bass.ds(h, 1), :, :].rearrange("a p n -> (a p) n")
                                 ).then_inc(decay_in, 16)
                    head_chunk(h, 4)
                    head_chunk(h, 5)

                head_chunk(0, 0)
                head_chunk(0, 1)
                sp.wait_ge(x_done, 1 + 2 * OUT_PAIRS)
                sp.dma_start(x_spill, x_sb[:]).then_inc(spill_done, 16)
                sp.wait_ge(xn_done, 1 + 2 * KT)
                sp.wait_ge(spill_done, 16)
                sp.dma_start(freq[:], ins["inv_freq"]).then_inc(rot_in, 16)
                sp.dma_start(cos[:].bitcast(I32), pos_d.broadcast_to([P, L])).then_inc(rot_in, 16)
                with sp.Fori(0, HEADS - 1) as h:
                    head(h)
                    head_chunk(h + 1, 0)
                    head_chunk(h + 1, 1)
                head(HEADS - 1)
                out_chunk(0, 0)
                out_chunk(0, 1)
                sp.wait_ge(a_lo_done, 1 + HEADS * 2)
                sp.dma_start(x_sb[:], x_spill).then_inc(back_done, 16)
                with sp.Fori(1, OUT_PAIRS) as dp:
                    out_chunk(dp, 0)
                    out_chunk(dp, 1)

            def s5():
                def glu_pair(i, dp0):
                    for k in range(2):
                        load(i * 2 + (C_GLU + 2 * dp0 + k), k, glu_w[:, :, bass.ds(i * CW + (dp0 * CW + (D, 0)[k]), CW)])
                glu_pair(0, 0)
                sp.wait_ge(x_done, 1 + 5 * OUT_PAIRS)
                for r, name in enumerate(("s5_a_re", "s5_a_im")):
                    for half in range(2):
                        sp.dma_start(a_nat[:, r, half * NS:(half + 1) * NS], ins[name][0]).then_inc(nat_in, 16)
                for r, name in enumerate(("s5_b_re", "s5_b_im")):
                    sp.dma_start(b_nat[:, r], ins[name][0].rearrange("g p k -> g (p k)")).then_inc(nat_in, 16)
                for r, name in enumerate(("s5_c_re", "s5_c_im")):
                    src = ins[name][0].rearrange("(b g) k p -> (g k) b p", g=GB)
                    for half in range(2):
                        sp.dma_start(c_nat[:, r, :, half * NS:(half + 1) * NS], src).then_inc(nat_in, 16)
                with sp.Fori(0, OUT_PAIRS - 1) as i:
                    glu_pair(i, 1)

            sp.dma_start(s5_const[:], ins["s5_const"]).then_inc(rows_in, 16)
            sp.dma_start(dt[:], ins["s5_log_dt"].broadcast_to([P, G])).then_inc(dt_in, 16)
            sp.dma_start(sq[0:72, 0, 0:P], ins["ada_b"][0].rearrange("(r n) -> r n", n=P)).then_inc(rows_in, 16)
            sp.dma_start(sq[0:72, 0, P:2 * P], ins["ada_b"][1].rearrange("(r n) -> r n", n=P)).then_inc(rows_in, 16)
            at = 0
            for src in (ins["norm_g"].rearrange("l s (r n) -> (l s r) n", n=P),
                        ins["final_g"].rearrange("(r n) -> r n", n=P),
                        ins["s5_d"].rearrange("l (r n) -> (l r) n", n=P),
                        c_d.rearrange("b (r n) -> (b r) n", n=P)):
                sp.dma_start(sq[at:at + src.shape[0], 0, 2 * P:3 * P], src).then_inc(rows_in, 16)
                at += src.shape[0]
            for q in range(ADA_FIRST):
                for half in range(2):
                    sp.dma_start(ada_first[:, q, 4 * half:4 * half + 4, :],
                                 ada_w[0][:, 4 * half:4 * half + 4, q * ADA_W:(q + 1) * ADA_W]
                                 ).then_inc(ada0_in[q], 16)
            ffn(0)
            retention()
            ffn(1)
            ffn(2)
            s5()
            ffn(3)
            sp.wait_ge(y_copied, KT)
            out_v = out.rearrange("b (t p) n -> p (b t) n", p=P)
            sp.dma_start(out_v, x_tok[:]).then_inc(stored, 16)
            sp.wait_ge(stored, 16)

        @block.gpsimd
        def _(pool):
            nc.gpsimd.memset(ident[:], 0.0).then_inc(consts, 1)
            nc.gpsimd.memset(ones[:], 1.0).then_inc(consts, 1)
            nc.gpsimd.memset(mhalf[:], -0.5).then_inc(consts, 1)
            nc.gpsimd.memset(rho[:], float(np.e)).then_inc(consts_e, 1)
            pool.wait_ge(consts, 3)
            nc.gpsimd.affine_select(out=ident[:], in_=ident[:], compare_op=ALU.not_equal, fill=1.0, base=0,
                                    pattern=[[-1, P]], channel_multiplier=1).then_inc(consts, 1)
            pool.wait_ge(consts_e, 1)
            pool.wait_ge(dt_in, 16)
            nc.gpsimd.tensor_tensor(dt[:], rho[:], dt[:], ALU.pow).then_inc(exp_done, 1)

            def norm(k):
                pool.wait_ge(ms_done, k + 1)
                nc.gpsimd.tensor_tensor(rstd[:], ms[:], mhalf[:], ALU.pow).then_inc(rstd_done, 1)

            def retention():
                with pool.Fori(0, HEADS) as h:
                    for I in range(TT):
                        pool.wait_ge(gn_var, h * TT + (I + 1))
                        nc.gpsimd.tensor_tensor(gn[:, I % 2, 1:2], gn[:, I % 2, 0:1], mhalf[:, 0:1],
                                                ALU.pow).then_inc(gn_rstd, 1)
            def s5():
                g, ps_ = nc.gpsimd, Steps(pool, pool_steps)

                def tt(o, a, b, op):
                    return ps_(g.tensor_tensor(o, a, b, op))
                half = slice(G // 2, G)
                c1, s1, t1, t2, ct, st = (a[:, half] for a in (small["c1"], small["s1"], small["t2"], small["half"],
                                                               ctab, stab))
                g.memset(ct[:, :, 0:1], 1.0).then_inc(zeroed, 1)
                g.memset(st[:, :, 0:1], 0.0).then_inc(zeroed, 1)
                pool.wait_ge(zeroed, 2)
                pool.wait_ge(turn_done, 1)
                n = 1
                while n < NC:
                    nb = lambda t: t.unsqueeze(2).broadcast_to([P, G // 2, n])
                    lo, hi, tmp = slice(0, n), slice(n, 2 * n), tab_tmp[:, half, 0:n]
                    tt(ct[:, :, hi], ct[:, :, lo], nb(c1), ALU.mult)
                    tt(tmp, st[:, :, lo], nb(s1), ALU.mult)
                    tt(st[:, :, hi], st[:, :, lo], nb(c1), ALU.mult)
                    ps_.wait()
                    tt(ct[:, :, hi], ct[:, :, hi], tmp, ALU.subtract)
                    ps_.wait()
                    tt(tmp, ct[:, :, lo], nb(s1), ALU.mult)
                    ps_.wait()
                    tt(st[:, :, hi], st[:, :, hi], tmp, ALU.add)
                    ps_.wait()
                    n *= 2
                    if n < NC:
                        tt(t1, s1, s1, ALU.mult)
                        tt(t2, s1, c1, ALU.mult)
                        tt(c1, c1, c1, ALU.mult)
                        ps_.wait()
                        tt(s1, t2, t2, ALU.add)
                        tt(c1, c1, t1, ALU.subtract)
                        ps_.wait()
                g.sem_inc(tabs_half, 1)
                pool.wait_ge(tabs_done, 1)
                g.memset(s_prev[:], 0.0).then_inc(zeroed, 1)
                g.memset(mt[:], 0.0).then_inc(zeroed, 1)
                g.sem_inc(xs_step, 1)
                def inputs_powers(b):
                    if not (isinstance(b, int) and b == 0):
                        pool.wait_ge(xs_turned, b)
                        pool.wait_ge(rows_done, b)
                    for hf in range(2):
                        gs = bass.ds(b * GB + hf * (GB // 2), GB // 2)
                        shape = [P, GB // 2, SC, SK]
                        xh = xs[:, hf * (GB // 2):(hf + 1) * (GB // 2)]
                        pool.wait_ge(xs_step, b * 6 + (3 * hf + 1))
                        g.tensor_tensor(xh, b_re[:, gs, :].unsqueeze(2).broadcast_to(shape),
                                        pw1[:, gs, 0:SC].unsqueeze(3).broadcast_to(shape),
                                        ALU.mult).then_inc(xs_step, 1)
                        g.tensor_tensor(xt[:], b_im[:, gs, :].unsqueeze(2).broadcast_to(shape),
                                        pw2[:, gs, 0:SC].unsqueeze(3).broadcast_to(shape),
                                        ALU.mult).then_inc(xs_step, 1)
                        pool.wait_ge(xs_step, b * 6 + (3 * hf + 3))
                        g.tensor_tensor(xh, xh, xt[:], ALU.add).then_inc(xs_step, 1)
                    pool.wait_ge(xs_step, b * 6 + 7)
                    g.sem_inc(xs_done, 1)

                inputs_powers(0)
                with pool.Fori(1, KT) as b:
                    inputs_powers(b)

            norm(0)
            norm(1)
            retention()
            norm(2)
            norm(3)
            norm(4)
            s5()
            norm(5)
            norm(6)

        @block.scalar
        def _(act):
            st = Steps(act, act_steps)
            copy = lambda o, i: nc.scalar.activation(o, i, ACT.Copy)

            def split_hi(n, k, r=8):
                act.wait_ge(w_landed[k % 2], landed(n, k))
                act.wait_ge(w_used, n)
                copy(w_hi[k % 2][:, 0:r, :], w_raw[k % 2][:, 0:r, :]).then_inc(w_hi_done, 1)

            def norm(k, shift, plain=None):
                for t in range(KT):
                    act.wait_ge(xn_done, 1 + KT * k + t + 1)
                    if plain is None:
                        nc.scalar.activation(slots[t % 4], slots[t % 4], ACT.Identity,
                                             bias=mods[:, shift + t:shift + t + 1],
                                             scale=scale1[:, t:t + 1]).then_inc(hf_done, 1)
                        act.wait_ge(hf_done, KT * k + t + 1)
                        copy(h_hi[:, t], slots[t % 4]).then_inc(h_hi_done, 1)
                    elif plain == "u":
                        nc.scalar.activation(u[:, t], slots[t % 4], ACT.Identity,
                                             bias=mods[:, shift + t:shift + t + 1],
                                             scale=scale1[:, t:t + 1]).then_inc(hf_done, 1)
                    else:
                        nc.scalar.activation(slots[t % 4], slots[t % 4], ACT.Identity,
                                             scale=par[:, COL_FG + t:COL_FG + t + 1]).then_inc(hf_done, 1)
                        act.wait_ge(y_turned, t + 1)
                        copy(x_tok[:, :, t * P:(t + 1) * P],
                             ps[:, t % 2, :].rearrange("p (t n) -> p t n", t=TT)).then_inc(y_copied, 1)

            def square(pair, tiles):
                act.wait_ge(x_done, pair + 2)
                act.wait_ge(acc_done, pair + 1)
                nc.scalar.activation(sq[:], x_sb[:, tiles, :], ACT.Square).then_inc(sq_done, 1)

            def out_phase(n0, chunks, pair0, last=False, begun=False):
                m = len(chunks)
                def body(j, last, begun=False):
                    n = j * (2 * m) + n0
                    for dp in range(2):
                        for c in range(m):
                            k = dp * m + c
                            if not (last and k == 2 * m - 1) and not (begun and k == 0):
                                nr = chunks[(c + 1) % m]
                                split_hi(n + (k + 1), k + 1, nr)
                        square(j * 2 + (pair0 + dp), bass.ds(j * 4 + 2 * dp, 2))
                if last or begun:
                    body(0, False, begun)
                    body(1, last)
                else:
                    with act.Fori(0, 2) as j:
                        body(j, False)

            def ffn(f, last=False):
                n0 = C_FFN[f]
                def in_pair(i):
                    n = i * 2 + n0
                    split_hi(n + 1, 1)
                    act.wait_ge(w_used, n + 2)
                    act.wait_ge(g_lo_done, i + (FFN_PAIRS * f + 1))
                    nc.scalar.activation(s_buf[:], ps[:, 0:2], ACT.Silu).then_inc(silu_done, 1)
                    split_hi(n + 2, 0)
                    act.wait_ge(prod_done, i + (FFN_PAIRS * f + 2))
                    copy(g_hi[:, bass.ds(i * 2, 2), :], s_buf[:]).then_inc(g_hi_done, 1)
                with act.Fori(0, ADA_IN) as i:
                    in_pair(i)
                in_pair(ADA_IN)
                out_phase(n0 + 2 * FFN_PAIRS, FFN_OUT, OUT_PAIRS * (SUB[f] + 1), last)

            def retention():
                split_hi(C_RET + 1, 1)
                act.wait_ge(ang_done, 1)
                nc.scalar.activation(sin[:], sq[:, 0], ACT.Sin).then_inc(trig_done, 1)
                nc.scalar.activation(cos[:], sq[:, 1], ACT.Sin).then_inc(trig_done, 1)
                with act.Fori(0, HEADS) as h:
                    n = h * 6 + C_RET
                    for k in range(2):
                        if k:
                            split_hi(n + 2, 2)
                        act.wait_ge(rot_done, h * 2 + (k + 1))
                        copy((q_hi, k_hi)[k][:, 0:2, :], s_buf[:]).then_inc(rot_hi_done, 1)
                    split_hi(n + 3, 3)
                    v_part(h, n, 0)
                    scores_hi(h, 0)
                    split_hi(n + 4, 4)
                    v_part(h, n, 1)
                    scores_hi(h, 1)
                    split_hi(n + 5, 5)
                    scores_hi(h, 2)
                    act.wait_ge(a_lo_done, h * 2 + 1)
                    turned_output(h, 0)
                    scores_hi(h, 3)
                    turned_output(h, 1)
                    split_hi(n + 6, 6)
                    turned_output(h, 2)
                    act.wait_ge(w_used, n + 7)
                    act.wait_ge(s_lo_done, h * TT + TT)
                    act.wait_ge(o_turned, h * TT + (TT + 1))
                    for pr, into in enumerate((s_buf, sq)):
                        nc.scalar.activation(into[:], ps[:, 4 + 2 * pr:6 + 2 * pr], ACT.Silu).then_inc(silu_g_done, 1)
                        if pr == 0:
                            turned_output(h, TT - 1)
                    for pr in range(2):
                        act.wait_ge(gated, h * 2 + (pr + 1))
                        copy(g_hi[:, bass.ds(h * TT + 2 * pr, 2), :], o_t[:, 2 * pr:2 * pr + 2, :]).then_inc(a_hi_done, 1)
                    split_hi(n + 7, 7)

            def v_part(h, n, e):
                act.wait_ge(w_used, n + (e + 4))
                copy(v_hi[:, :, e * CW:(e + 1) * CW],
                     ps[:, 4 + 2 * e:6 + 2 * e].rearrange("p b (t n) -> p (b t) n", t=2)).then_inc(v_hi_done, 1)

            def turned_output(h, I):
                act.wait_ge(o_turned, h * TT + (I + 2))
                copy(o_t[:, :, I * P:(I + 1) * P], ps[:, 3].rearrange("p (t n) -> p t n", t=TT)).then_inc(o_t_done, 1)

            def scores_hi(h, I):
                act.wait_ge(masked, h * TT + (I + 2))
                W = (I + 1) * P
                copy(s_hi[:, 0:W], s_buf[:, 1, 0:W]).then_inc(s_hi_done, 1)

            def s5():
                A = nc.scalar.activation
                for r, t in enumerate((b_re, b_im)):
                    act.wait_ge(nat_turned, r + 2)
                    for half in range(2):
                        ins = copy(t[half * NS:(half + 1) * NS],
                                   ps[0:NS, 2 * r:2 * r + 2].rearrange("p a (k g) -> p g (a k)", g=G))
                    ins.then_inc(nat_copied, 1)
                for r, t in enumerate((c_re, c_im)):
                    act.wait_ge(nat_turned, r + 4)
                    A(t[:].rearrange("p g k -> p (g k)"), ps[:, 4 + 2 * r:6 + 2 * r].rearrange("p a n -> p (a n)"),
                      ACT.Identity, scale=sgn).then_inc(nat_copied, 1)
                act.wait_ge(wave_in, 1)
                A(small["sh"], small["half"], ACT.Sin)
                A(small["ch"], small["arg"], ACT.Sin)
                A(small["tn"], small["x"], ACT.Tanh, scale=0.5).then_inc(wave_done, 1)
                act.wait_ge(tabs_done, 1)
                act.sem_inc(yz_done, 1)

                def tokens(b, first=False):
                    if not first:
                        act.wait_ge(u_turned, b)
                    copy(s_buf[:, 1], u[:, bass.ds(b, 1), :].rearrange("p a n -> p (a n)")).then_inc(ub_done, 1)
                    act.wait_ge(xs_done, b + 1)
                    if not first:
                        act.wait_ge(lag_done, b)
                    copy(b_rows[:].rearrange("p g (j k) -> p g j k", k=SK),
                         xs[:, :, 0:1, :].broadcast_to([P, GB, SC, SK])).then_inc(rows_done, 1)

                def front(b, s, first=False):
                    act.wait_ge(u_turned, b + 1)
                    if not first:
                        act.wait_ge(yz_turned, b)
                    copy(zt[:].rearrange("c (g j k) -> c j g k", g=GB, j=SC),
                         ps[0:NC, 0:2].rearrange("c a (j g k) -> c (a j) g k", g=GB, k=SK)).then_inc(z_done, 1)
                    act.wait_ge(xs_turned, b + 1)
                    if not first:
                        act.wait_ge(v_done, b)
                    copy(win[:].rearrange("p g n -> p (g n)"), ps[:, 3:5].rearrange("p a n -> p (a n)")
                         ).then_inc(win_done, 1)
                    act.wait_ge(lag_done, b + 1)
                    if not first:
                        act.wait_ge(y_done, b)
                    for J in range(4):
                        q = slice(32 * J, 32 * J + 32)
                        w = (2 * J + 2) * SK
                        ins = A(mt[q, s, :, P - w:P], ps[q, 5:7].rearrange("p a (g n) -> p (a g) n", n=P)[:, :, 0:w],
                                ACT.Copy, scale=odd[q])
                    ins.then_inc(m_early, 1)

                def back(b, after=False):
                    act.wait_ge(y_done, b + 2)
                    copy(zt[:].rearrange("c (i g k) -> c g i k", g=GB, i=SC),
                         ps[0:NC, 0:2].rearrange("c a (g i k) -> c (a g) i k", i=SC, k=SK)).then_inc(yz_done, 1)
                    if after:
                        tokens(b + 2)
                    act.wait_ge(yd_done, b + 2)
                    A(s_buf[:, 0], s_buf[:, 0], ACT.Gelu_apprx_tanh).then_inc(gelu_done, 1)
                    act.wait_ge(gelu_done, b + 1)
                    copy(h_hi[:, bass.ds(b, 1), :].rearrange("p a n -> p (a n)"), s_buf[:, 0]).then_inc(a5_hi, 1)

                tokens(0, True)
                front(0, 0, True)
                tokens(1)
                with act.Fori(0, KT // 2 - 1) as i:
                    for s in range(2):
                        front(i * 2 + (s + 1), 1 - s)
                        back(i * 2 + s, True)
                front(KT - 1, 1)
                back(KT - 2)
                back(KT - 1)
                with act.Fori(0, OUT_PAIRS) as dp:
                    n = dp * 2 + C_GLU
                    split_hi(n + 1, 1)
                    act.wait_ge(w_used, n + 2)
                    act.wait_ge(x_done, dp + (5 * OUT_PAIRS + 1))
                    A(s_buf[:], ps[:, 0:2], ACT.Sigmoid).then_inc(gate_done, 1)
                    split_hi(n + 2, 0)
                    square(dp + 5 * OUT_PAIRS, bass.ds(dp * 2, 2))

            act.sem_inc(w_hi_done, 1)
            act.sem_inc(silu_done, 1)
            act.sem_inc(silu_g_done, 1)
            act.sem_inc(o_t_done, 1)
            for t in range(TT):
                act.dma_start(x_tok[:, t], x_d[0].rearrange("(t p) n -> p t n", p=P)[:, t]).then_inc(x_in[t], 16)
            act.wait_ge(par_done, 1)
            nc.scalar.activation(csil[:], par[:, COL_C:COL_C + KT], ACT.Silu).then_inc(csil_done, 1)
            for pr in range(OUT_PAIRS):
                act.wait_ge(x_turned, 2 * pr + 2)
                copy(x_sb[:, 2 * pr:2 * pr + 2], ps[:, (2 * pr) % 4:(2 * pr) % 4 + 2]).then_inc(x_copied, 1)
                act.wait_ge(x_copied, pr + 1)
                if pr:
                    act.wait_ge(acc_done, pr + 1)
                nc.scalar.activation(sq[:], x_sb[:, 2 * pr:2 * pr + 2], ACT.Square).then_inc(sq_done, 1)
            act.wait_ge(w_landed[0], 16)
            copy(w_hi[0][:], w_raw[0][:]).then_inc(w_hi_done, 1)
            norm(0, 0)
            ffn(0)
            norm(1, 3 * KT)
            retention()
            out_phase(C_RET_OUT, RET_OUT, OUT_PAIRS * 2, begun=True)
            norm(2, 6 * KT)
            ffn(1)
            norm(3, 9 * KT)
            ffn(2)
            norm(4, 12 * KT, "u")
            s5()
            norm(5, 15 * KT)
            ffn(3, True)
            norm(6, 0, "out")

        @block.vector
        def _(dve):
            st = Steps(dve, dve_steps)
            V = nc.vector

            def split_lo(n, k, r=8):
                dve.wait_ge(w_hi_done, n + 2)
                V.tensor_tensor(w_lo[k % 2][:, 0:r, :], w_raw[k % 2][:, 0:r, :],
                                raw_f32(w_hi[k % 2][:, 0:r, :]), ALU.subtract).then_inc(w_lo_done, 1)

            def ada_terms(raw, c0, into, first):
                for t in range(raw.shape[1]):
                    c = csil[:, c0 + t:c0 + t + 1]
                    if first and t == 0:
                        st(V.tensor_scalar(into, raw[:, t], c, None, ALU.mult))
                    else:
                        st.wait()
                        st(V.scalar_tensor_tensor(out=into, in0=raw[:, t], scalar=c, in1=into,
                                                  op0=ALU.mult, op1=ALU.add))

            def ada_step(Q):
                dve.wait_ge(ada_summed, Q + ADA_FIRST)
                for p in range(4):
                    dve.wait_ge(ada_landed[p % 2], Q * 32 + (16 + 16 * (p // 2)))
                    ada_terms(ada_raw[:, p % 2], 2 * p, ada_acc[:], p == 0)
                    st.wait()
                    dve.sem_inc(ada_used, 1)
                dve.sem_inc(ada_acc_done, 1)

            def ada_bias(Q):
                dve.wait_ge(ada_summed, Q + (ADA_FIRST + 1))
                at = bass.ds(Q * 4 + 4 * ADA_FIRST, 4)
                V.tensor_tensor(mods[:, at], ps[:, 6, 0:4], par[:, at], ALU.add).then_inc(mods_done, 1)

            def add_squares(pair):
                dve.wait_ge(sq_done, pair + 1)
                for t in range(2):
                    st.wait()
                    ins = st(V.tensor_tensor(acc[:], acc[:], sq[:, t], ALU.add))
                st.wait()
                dve.sem_inc(acc_done, 1)

            def norm(k, l, s, kind="h"):
                if kind != "out":
                    dve.wait_ge(mods_done, MODS_NEED[k])
                    c = (l * N_MOD + 3 * s + 1) * KT
                    g = COL_G + (3 * l + s) * KT
                    V.scalar_tensor_tensor(out=scale1[:], in0=mods[:, c:c + KT], scalar=1.0, in1=par[:, g:g + KT],
                                           op0=ALU.add, op1=ALU.mult)
                dve.wait_ge(stat_done, k + 1)
                V.tensor_scalar(ms[:], ps[:, 4, 0:TT], 1.0 / D, NORM_EPS, ALU.mult, ALU.add).then_inc(ms_done, 1)
                st(V.memset(acc[:], 0.0))
                dve.wait_ge(rbc_done, k + 1)

                def lo(t):
                    dve.wait_ge(h_hi_done, HK[k] * KT + t + 1)
                    V.tensor_tensor(h_lo[:, t], slots[t % 4], raw_f32(h_hi[:, t]),
                                    ALU.subtract).then_inc(h_lo_done, 1)
                for t in range(KT):
                    if t >= 2:
                        if kind == "h":
                            lo(t - 2)
                    if t >= 4:
                        if kind == "h":
                            dve.wait_ge(h_lo_done, HK[k] * KT + t - 3)
                        elif kind == "u":
                            dve.wait_ge(hf_done, KT * k + t - 3)
                        else:
                            dve.wait_ge(y_turned, t - 3)
                    V.tensor_tensor(slots[t % 4], x_sb[:, t], ps[:, 5], ALU.mult).then_inc(xn_done, 1)
                if kind == "h":
                    lo(KT - 2)
                    lo(KT - 1)

            def set_coef(l, s, factor, need):
                dve.wait_ge(mods_done, need)
                c = (l * N_MOD + 3 * s + 2) * KT
                st(V.tensor_scalar(coef[:], mods[:, c:c + KT], factor, None, ALU.mult))

            def residual(j, dp, banks):
                st.wait()
                for t in range(2):
                    tile = bass.ds(j * 4 + (2 * dp + t), 1)
                    ins = V.scalar_tensor_tensor(out=x_sb[:, tile, :], in0=ps[:, banks + t:banks + t + 1, :],
                                                 scalar=coef[:, tile], in1=x_sb[:, tile, :],
                                                 op0=ALU.mult, op1=ALU.add)
                ins.then_inc(x_done, 1)

            def out_phase(n0, chunks, pair0, last=False, ada=None, begun=False):
                m = len(chunks)
                def body(j, last, begun=False):
                    n = j * (2 * m) + n0
                    for dp in range(2):
                        for c in range(m):
                            k = dp * m + c
                            if not (last and k == 2 * m - 1) and not (begun and k == 0):
                                split_lo(n + (k + 1), k + 1, chunks[(c + 1) % m])
                            if ada is not None and c == 1:
                                ada_step(j * 2 + (ada + dp))
                        dve.wait_ge(w_used, n + (k + 2))
                        residual(j, dp, 2 * dp)
                        if ada is not None:
                            ada_bias(j * 2 + (ada + dp))
                        add_squares(j * 2 + (pair0 + dp))
                per = 4 + (16 if ada is not None else 0)
                if last or begun:
                    body(0, False, begun)
                    body(1, last)
                else:
                    with st.loop(2, per) as j:
                        body(j, False)

            def ffn(f, last=False):
                n0 = C_FFN[f]
                a_in, a_out = ADA_AT[f]
                def in_pair(i, ada):
                    n = i * 2 + n0
                    split_lo(n + 1, 1)
                    if ada:
                        ada_step(i + a_in)
                    split_lo(n + 2, 0)
                    dve.wait_ge(w_used, n + 3)
                    dve.wait_ge(silu_done, i + (FFN_PAIRS * f + 2))
                    V.tensor_tensor(s_buf[:], s_buf[:], ps[:, 2:4], ALU.mult).then_inc(prod_done, 1)
                    if ada:
                        ada_bias(i + a_in)
                    dve.wait_ge(g_hi_done, i + (FFN_PAIRS * f + 1))
                    V.tensor_tensor(g_lo[:, bass.ds(i * 2, 2), :], s_buf[:], raw_f32(g_hi[:, bass.ds(i * 2, 2), :]),
                                    ALU.subtract).then_inc(g_lo_done, 1)
                ada = a_in is not None
                with st.loop(ADA_IN, 8 if ada else 0) as i:
                    in_pair(i, ada)
                in_pair(ADA_IN, False)
                set_coef(f // 2, 2 * (f % 2), 0.5, (14, 28, 32, 36)[f])
                out_phase(n0 + 2 * FFN_PAIRS, FFN_OUT, OUT_PAIRS * (SUB[f] + 1), last, a_out)

            def reduce_turns(ang, cnt):
                turn, magic = 2 * np.pi, 1.5 * 2.0 ** 23
                parts, rest = [], turn
                for bits in (5, 13, 21):
                    parts.append(float(np.floor(rest * 2.0 ** bits) / 2.0 ** bits))
                    rest -= parts[-1]
                parts.append(float(np.float32(rest)))
                st(V.tensor_scalar(cnt, ang, 1.0 / turn, None, ALU.mult))
                st.wait()
                st(V.tensor_scalar(cnt, cnt, magic, None, ALU.add))
                st.wait()
                st(V.tensor_scalar(cnt, cnt, magic, None, ALU.subtract))
                st.wait()
                for part in parts:
                    st(V.scalar_tensor_tensor(out=ang, in0=cnt, scalar=-part, in1=ang, op0=ALU.mult, op1=ALU.add))
                    st.wait()
                lim = float(np.nextafter(np.float32(np.pi), np.float32(0)))
                st(V.tensor_scalar(ang, ang, lim, -lim, ALU.min, ALU.max))
                st.wait()

            def angles():
                dve.wait_ge(rot_in, 32)
                posf, ang, cnt = s_buf[:, 0], sq[:, 0], s_buf[:, 1]
                st(V.tensor_copy(posf, cos[:].bitcast(I32)))
                st.wait()
                st(V.tensor_scalar(ang, posf, freq[:], None, ALU.mult))
                st.wait()
                reduce_turns(ang, cnt)
                st(V.tensor_scalar(sq[:, 1], ang, -1.0, None, ALU.mult))
                st.wait()
                st(V.tensor_tensor(sq[:, 1], sq[:, 1], ang, ALU.min))
                st.wait()
                V.tensor_scalar(sq[:, 1], sq[:, 1], float(np.float32(np.pi / 2)), None, ALU.add).then_inc(ang_done, 1)

            def retention():
                split_lo(C_RET + 1, 1)
                angles()
                dve.wait_ge(trig_done, 2)
                with st.loop(HEADS, 12 + 8) as h:
                    n = h * 6 + C_RET
                    for k in range(2):
                        if k:
                            split_lo(n + 2, 2)
                        dve.wait_ge(w_used, n + (k + 2))
                        dve.wait_ge(a_lo_done, h * 2 + 1)
                        t1, t2 = ps[:, 2 * k], ps[:, 2 * k + 1]
                        st.wait()
                        st(V.tensor_tensor(sq[:, 0], t1, cos[:], ALU.mult))
                        st(V.tensor_tensor(sq[:, 1], t2, sin[:], ALU.mult))
                        dve.wait_ge(rot_lo_done, h * 2 + (k + 1))
                        st(V.tensor_tensor(s_buf[:, 1], t1, sin[:], ALU.mult))
                        st.wait()
                        st(V.tensor_tensor(s_buf[:, 0], sq[:, 0], sq[:, 1], ALU.subtract))
                        st.wait()
                        st(V.tensor_tensor(sq[:, 0], t2, cos[:], ALU.mult))
                        st.wait()
                        st(V.tensor_tensor(s_buf[:, 1], s_buf[:, 1], sq[:, 0], ALU.add))
                        st.wait()
                        dve.sem_inc(rot_done, 1)
                        dve.wait_ge(rot_hi_done, h * 2 + (k + 1))
                        hi, lo = ((q_hi, q_lo), (k_hi, k_lo))[k]
                        V.tensor_tensor(lo[:, 0:2, :], s_buf[:], raw_f32(hi[:, 0:2, :]),
                                        ALU.subtract).then_inc(rot_lo_done, 1)
                    split_lo(n + 3, 3)
                    v_part_lo(h, 0)
                    scores_masked(h, 0)
                    split_lo(n + 4, 4)
                    v_part_lo(h, 1)
                    scores_masked(h, 1)
                    normed(h, 0)
                    split_lo(n + 5, 5)
                    scores_masked(h, 2)
                    normed(h, 1)
                    scores_masked(h, 3)
                    normed(h, 2)
                    split_lo(n + 6, 6)
                    normed(h, 3)
                    dve.wait_ge(o_t_done, h * TT + (TT + 1))
                    for pr, gate in enumerate((s_buf, sq)):
                        dve.wait_ge(silu_g_done, h * 2 + (pr + 2))
                        V.tensor_tensor(o_t[:, 2 * pr:2 * pr + 2, :], o_t[:, 2 * pr:2 * pr + 2, :], gate[:],
                                        ALU.mult).then_inc(gated, 1)
                    for pr in range(2):
                        dve.wait_ge(a_hi_done, h * 2 + (pr + 1))
                        a = bass.ds(h * TT + 2 * pr, 2)
                        V.tensor_tensor(g_lo[:, a, :], o_t[:, 2 * pr:2 * pr + 2, :], raw_f32(g_hi[:, a, :]),
                                        ALU.subtract).then_inc(a_lo_done, 1)
                    split_lo(n + 7, 7)

            def v_part_lo(h, e):
                dve.wait_ge(v_hi_done, h * 2 + (e + 1))
                V.tensor_tensor(v_lo[:, :, e * CW:(e + 1) * CW],
                                ps[:, 4 + 2 * e:6 + 2 * e].rearrange("p b (t n) -> p (b t) n", t=2),
                                raw_f32(v_hi[:, :, e * CW:(e + 1) * CW]), ALU.subtract).then_inc(v_lo_done, 1)

            def normed(h, I):
                E = h * TT + I
                pv = ps[:, 1 + I % 2]
                dve.wait_ge(pv_done, E + 1)
                st(V.bn_stats(bn[:, 0, 0:6], pv))
                st.wait()
                dve.sem_inc(bn_ready, 1)
                st(V.bn_aggr(bn[:, 1, 0:2], bn[:, 0, 0:6]))
                st.wait()
                V.tensor_scalar(gn[:, I % 2, 0:1], bn[:, 1, 1:2], GN_EPS, None, ALU.add).then_inc(gn_var, 1)
                dve.wait_ge(gn_rstd, E + 1)
                dve.wait_ge(o_turned, E + 1)
                V.tensor_scalar(o_n, pv, bn[:, 1, 0:1], gn[:, I % 2, 1:2],
                                ALU.subtract, ALU.mult).then_inc(o_normed, 1)

            def scores_masked(h, I):
                E = h * TT + I
                W = (I + 1) * P
                dve.wait_ge(score_done, E + 1)
                if I == 0:
                    dve.wait_ge(decay_in, h * 16 + 16)
                for J in range(I + 1):
                    c = (I - J) * P
                    ins = V.tensor_tensor(s_buf[:, 1, J * P:(J + 1) * P], ps[:, 0, J * P:(J + 1) * P],
                                          decay[:, c:c + P], ALU.mult)
                ins.then_inc(masked, 1)
                dve.wait_ge(s_hi_done, E + 1)
                V.tensor_tensor(s_lo[:, 0:W], s_buf[:, 1, 0:W], raw_f32(s_hi[:, 0:W]),
                                ALU.subtract).then_inc(s_lo_done, 1)

            def s5():
                S = small
                dve.wait_ge(hf_done, 5 * KT)
                tt = lambda o, a, b, op: st(V.tensor_tensor(o, a, b, op))
                ts = lambda o, a, x, y, f, g: st(V.tensor_scalar(o, a, x, y, f, g))

                def w(*_):
                    st.wait()
                M, A_, Sb = ALU.mult, ALU.add, ALU.subtract
                dve.wait_ge(nat_turned, 1)
                st(V.tensor_copy(S["are"], ps[:, 7, 0:G]))
                st(V.tensor_copy(S["aim"], ps[:, 7, G:2 * G]))
                w()
                dve.sem_inc(a_copied, 1)
                dve.wait_ge(exp_done, 1)
                tt(S["x"], S["are"], dt[:], M)
                tt(S["th"], S["aim"], dt[:], M)
                w()
                dve.sem_inc(bank7_read, 1)
                reduce_turns(S["th"], S["cnt"])
                ts(S["half"], S["th"], 0.5, None, M, ALU.bypass)
                ts(S["arg"], S["th"], -0.5, None, M, ALU.bypass)
                w()
                tt(S["arg"], S["arg"], S["half"], ALU.min)
                w()
                ts(S["arg"], S["arg"], float(np.float32(np.pi / 2)), None, A_, ALU.bypass)
                w()
                dve.sem_inc(wave_in, 1)
                dve.wait_ge(wave_done, 1)
                ts(S["t2"], S["tn"], -1.0, 1.0, M, A_)
                w()
                st(V.reciprocal(S["t2"], S["t2"]))
                tt(S["s1"], S["sh"], S["ch"], M)
                tt(S["w"], S["sh"], S["sh"], M)
                w()
                st(V.scalar_tensor_tensor(out=S["em1"], in0=S["tn"], scalar=2.0, in1=S["t2"], op0=M, op1=M))
                ts(S["s1"], S["s1"], 2.0, None, M, ALU.bypass)
                ts(S["w"], S["w"], 2.0, None, M, ALU.bypass)
                w()
                ts(S["ex"], S["em1"], 1.0, None, A_, ALU.bypass)
                ts(S["c1"], S["w"], -1.0, 1.0, M, A_)
                w()
                tt(S["nre"], S["em1"], S["c1"], M)
                tt(S["nim"], S["ex"], S["s1"], M)
                tt(rho[:], S["ex"], S["ex"], M)
                w()
                tt(rho[:], rho[:], rho[:], M)
                w()
                tt(rho[:], rho[:], rho[:], M)
                tt(S["nre"], S["nre"], S["w"], Sb)
                tt(S["fre"], S["are"], S["are"], M)
                tt(S["fim"], S["aim"], S["aim"], M)
                w()
                tt(S["cnt"], S["fre"], S["fim"], A_)
                tt(S["t2"], S["nre"], S["are"], M)
                tt(S["half"], S["nim"], S["aim"], M)
                tt(S["arg"], S["nim"], S["are"], M)
                tt(S["tn"], S["nre"], S["aim"], M)
                w()
                st(V.reciprocal(S["cnt"], S["cnt"]))
                tt(S["t2"], S["t2"], S["half"], A_)
                tt(S["arg"], S["arg"], S["tn"], Sb)
                w()
                tt(S["fre"], S["t2"], S["cnt"], M)
                tt(S["fim"], S["arg"], S["cnt"], M)
                ts(S["a"], S["nre"], 1.0, None, A_, ALU.bypass)
                st(V.tensor_copy(S["b"], S["nim"]))
                def square_turn(q):
                    tt(S["t2"][:, q], S["s1"][:, q], S["s1"][:, q], M)
                    tt(S["half"][:, q], S["s1"][:, q], S["c1"][:, q], M)
                    w()
                    ts(S["c1"][:, q], S["t2"][:, q], -2.0, 1.0, M, A_)
                    ts(S["s1"][:, q], S["half"][:, q], 2.0, None, M, ALU.bypass)
                    w()
                ts(S["s1"], S["s1"], sgn, None, M, ALU.bypass)
                w()
                for _ in range(3):
                    square_turn(slice(0, G))
                dve.sem_inc(turn_done, 1)
                st(V.memset(pw1[0:NS, :, 0], 1.0))
                st(V.memset(pw1[NS:P, :, 0], 0.0))
                st(V.memset(pw2[0:NS, :, 0], 0.0))
                st(V.memset(pw2[NS:P, :, 0], 1.0))
                w()
                for d in range(SC):
                    tt(S["x"], S["a"], pw1[:, :, d], M)
                    tt(S["cnt"], S["b"], pw2[:, :, d], M)
                    tt(S["th"], S["a"], pw2[:, :, d], M)
                    tt(S["arg"], S["b"], pw1[:, :, d], M)
                    w()
                    tt(pw1[:, :, d + 1], S["x"], S["cnt"], A_)
                    tt(pw2[:, :, d + 1], S["th"], S["arg"], Sb)
                    w()
                dve.wait_ge(nat_copied, 4)
                kb = lambda t: t.unsqueeze(2).broadcast_to([P, G, SK])
                sbb = s_buf[:].rearrange("p a (g k) -> p (a g) k", k=SK)
                tt(sbb, b_im[:], kb(S["fim"]), M)
                tt(bb_tmp[:], b_re[:], kb(S["fim"]), M)
                w()
                tt(b_re[:], b_re[:], kb(S["fre"]), M)
                tt(b_im[:], b_im[:], kb(S["fre"]), M)
                w()
                tt(b_re[:], b_re[:], sbb, Sb)
                tt(b_im[:], b_im[:], bb_tmp[:], A_)
                first = slice(0, G // 2)
                c1, s1, ct, sn = (a[:, first] for a in (S["c1"], S["s1"], ctab, stab))
                st(V.memset(ct[:, :, 0:1], 1.0))
                st(V.memset(sn[:, :, 0:1], 0.0))
                w()
                n = 1
                while n < NC:
                    nb = lambda t: t.unsqueeze(2).broadcast_to([P, G // 2, n])
                    lo, hi, tmp = slice(0, n), slice(n, 2 * n), tab_tmp[:, first, 0:n]
                    tt(ct[:, :, hi], ct[:, :, lo], nb(c1), M)
                    tt(tmp, sn[:, :, lo], nb(s1), M)
                    tt(sn[:, :, hi], sn[:, :, lo], nb(c1), M)
                    w()
                    tt(ct[:, :, hi], ct[:, :, hi], tmp, Sb)
                    w()
                    tt(tmp, ct[:, :, lo], nb(s1), M)
                    w()
                    tt(sn[:, :, hi], sn[:, :, hi], tmp, A_)
                    w()
                    n *= 2
                    if n < NC:
                        square_turn(first)
                dve.sem_inc(tabs_done, 1)
                dve.wait_ge(tabs_half, 1)
                dve.wait_ge(zeroed, 4)
                v3 = lambda t: t.rearrange("p (g c) -> p g c", c=NC)
                yy, turned, rot, z = s_buf[:, 0], sq[:, 0], sq[:, 1], acc[:]
                dve.sem_inc(yd_done, 1)
                dve.sem_inc(a5_lo, 1)

                def output_powers(b, s):
                    if not (isinstance(b, int) and b < 2):
                        dve.wait_ge(y_done, b)
                    for half in range(2):
                        gs = bass.ds(b * GB + half * (GB // 2), GB // 2)
                        shape = [P, GB // 2, SC + 1, SK]
                        yh = ys[:, s, half * (GB // 2):(half + 1) * (GB // 2)]
                        if half:
                            w()
                        tt(yh, c_re[:, gs, :].unsqueeze(2).broadcast_to(shape),
                           pw1[:, gs, :].unsqueeze(3).broadcast_to(shape), M)
                        tt(yt[:], c_im[:, gs, :].unsqueeze(2).broadcast_to(shape),
                           pw2[:, gs, :].unsqueeze(3).broadcast_to(shape), M)
                        w()
                        tt(yh, yh, yt[:], A_)
                    w()
                    dve.sem_inc(ys_done, 1)

                def chunk_inputs(b, s):
                    dve.wait_ge(z_turned, b + 1)
                    V.tensor_copy(us[:, s].rearrange("p g c -> p (g c)"), ps[:, 2]).then_inc(us_done, 1)

                def odd_rows(b, s):
                    dve.wait_ge(m_early, b + 1)
                    for J in range(4):
                        q = slice(32 * J, 32 * J + 32)
                        wd = (2 * J + 1) * SK
                        ins = V.scalar_tensor_tensor(
                            out=mt[q, s, :, P - wd:P],
                            in0=ps[q, 5:7].rearrange("p a (g n) -> p (a g) n", n=P)[:, :, 0:wd],
                            scalar=even[q], in1=mt[q, s, :, P - wd:P], op0=M, op1=A_)
                    ins.then_inc(m_done, 1)

                def scan(b):
                    gs = bass.ds(b * GB, GB)
                    tt(v3(z), rho[:, gs].unsqueeze(2).broadcast_to([P, GB, NC]),
                       cmask.unsqueeze(1).broadcast_to([P, GB, NC]), M)
                    dve.wait_ge(v_done, b + 1)
                    tt(v3(turned)[0:NS], v3(ps[:, 7])[NS:P], stab[NS:P, gs, :], M)
                    tt(v3(turned)[NS:P], v3(ps[:, 7])[0:NS], stab[0:NS, gs, :], M)
                    tt(v3(rot), v3(ps[:, 7]), ctab[:, gs, :], M)
                    w()
                    tt(rot, rot, turned, Sb)
                    w()
                    st(V.tensor_tensor_scan(turned, z, rot, 0.0, M, A_))
                    w()
                    tt(v3(rot)[0:NS], v3(turned)[NS:P], stab[NS:P, gs, :], M)
                    tt(v3(rot)[NS:P], v3(turned)[0:NS], stab[0:NS, gs, :], M)
                    tt(v3(z), v3(turned), ctab[:, gs, :], M)
                    w()
                    if not (isinstance(b, int) and b == 0):
                        dve.wait_ge(y_done, b + 1)
                    tt(s_prev[:, :, 1:NC], v3(z)[:, :, 0:NC - 1], v3(rot)[:, :, 0:NC - 1], A_)
                    w()
                    dve.sem_inc(sp_done, 1)

                def skip(b):
                    dve.wait_ge(a5_lo, b + 1)
                    dve.wait_ge(yz_turned, b + 2)
                    V.scalar_tensor_tensor(out=yy.rearrange("p (c i) -> p c i", i=SC),
                                           in0=u[:, bass.ds(b, 1), :].rearrange("p a (c i) -> p (a c) i", i=SC),
                                           scalar=par[:, bass.ds(b + COL_D, 1)],
                                           in1=ps[:, 2].rearrange("p (i c) -> p c i", i=SC),
                                           op0=M, op1=A_).then_inc(yd_done, 1)

                def output_lo(b):
                    dve.wait_ge(a5_hi, b + 1)
                    V.tensor_tensor(h_lo[:, bass.ds(b, 1), :].rearrange("p a n -> p (a n)"), yy,
                                    raw_f32(h_hi[:, bass.ds(b, 1), :]).rearrange("p a n -> p (a n)"),
                                    Sb).then_inc(a5_lo, 1)

                output_powers(0, 0)
                chunk_inputs(0, 0)
                odd_rows(0, 0)
                scan(0)
                output_powers(1, 1)
                with st.loop(KT // 2 - 1, 32) as i:
                    for s in range(2):
                        b = i * 2 + s
                        chunk_inputs(i * 2 + (s + 1), 1 - s)
                        odd_rows(i * 2 + (s + 1), 1 - s)
                        scan(i * 2 + (s + 1))
                        skip(b)
                        output_powers(i * 2 + (s + 2), s)
                        output_lo(b)
                chunk_inputs(KT - 1, 1)
                odd_rows(KT - 1, 1)
                scan(KT - 1)
                skip(KT - 2)
                output_lo(KT - 2)
                skip(KT - 1)
                output_lo(KT - 1)
                w()
                st(V.memset(acc[:], 0.0))
                set_coef(1, 1, 1.0, 36)
                with st.loop(OUT_PAIRS, 4) as dp:
                    n = dp * 2 + C_GLU
                    split_lo(n + 1, 1)
                    split_lo(n + 2, 0)
                    dve.wait_ge(w_used, n + 3)
                    dve.wait_ge(gate_done, dp + 1)
                    tt(s_buf[:], s_buf[:], ps[:, 2:4], M)
                    w()
                    for t in range(2):
                        tile = bass.ds(dp * 2 + t, 1)
                        ins_ = V.scalar_tensor_tensor(out=x_sb[:, tile, :], in0=s_buf[:, t:t + 1, :],
                                                      scalar=coef[:, tile], in1=x_sb[:, tile, :], op0=M, op1=A_)
                    st(ins_)
                    w()
                    dve.sem_inc(x_done, 1)
                    add_squares(dp + 5 * OUT_PAIRS)

            for s in (w_lo_done, ada_used, ada_used, x_done, acc_done, xn_done, prod_done,
                      g_lo_done, masked, a_lo_done, v_lo_done, rot_lo_done):
                dve.sem_inc(s, 1)
            st(V.memset(acc[:], 0.0))
            dve.wait_ge(rows_turned, 1)
            V.tensor_copy(par[:], ps[:, 7, 0:3 * 72]).then_inc(par_done, 1)
            for pr in range(OUT_PAIRS):
                add_squares(pr)
                dve.sem_inc(x_done, 1)
            dve.wait_ge(csil_done, 1)
            for q in range(ADA_FIRST):
                dve.wait_ge(ada0_in[q], 32)
                if q:
                    dve.wait_ge(ada_summed, q)
                ada_terms(ada_first[:, q], 0, ada_acc[:], True)
                st.wait()
                dve.sem_inc(ada_acc_done, 1)
                dve.wait_ge(ada_summed, q + 1)
                V.tensor_tensor(mods[:, 4 * q:4 * q + 4], ps[:, 6, 0:4], par[:, 4 * q:4 * q + 4],
                                ALU.add).then_inc(mods_done, 1)
            dve.wait_ge(w_hi_done, 2)
            V.tensor_tensor(w_lo[0][:], w_raw[0][:], raw_f32(w_hi[0][:]), ALU.subtract).then_inc(w_lo_done, 1)
            norm(0, 0, 0)
            ffn(0)
            norm(1, 0, 1)
            retention()
            set_coef(0, 1, 1.0, 18)
            dve.wait_ge(back_done, 16)
            out_phase(C_RET_OUT, RET_OUT, OUT_PAIRS * 2, begun=True)
            norm(2, 0, 2)
            ffn(1)
            norm(3, 1, 0)
            ffn(2)
            norm(4, 1, 1, "u")
            s5()
            norm(5, 1, 2)
            ffn(3, True)
            norm(6, 0, 0, "out")

        @block.tensor
        def _(pe):
            def mm3(o, wh, wl, xh, xl, start, stop):
                nc.tensor.matmul(o, wl, xh, start=start, stop=False)
                nc.tensor.matmul(o, wh, xl, start=False, stop=False)
                return nc.tensor.matmul(o, wh, xh, start=False, stop=stop)

            def chunk(n, k, xh, xl, r0, r, bank, first, last, h_from=None):
                pe.wait_ge(w_lo_done, n + 2)
                s = k % 2
                for t in range(r):
                    if h_from is not None:
                        pe.wait_ge(h_lo_done, h_from + t + 1)
                    for c in range(2):
                        m = mm3(ps[:, bank + c], w_hi[s][:, t, c * P:(c + 1) * P], w_lo[s][:, t, c * P:(c + 1) * P],
                                xh[:, r0 + t], xl[:, r0 + t], first and t == 0, last and t == r - 1)
                m.then_inc(w_used, 1)

            def ada_sum(Q):
                pe.wait_ge(ada_acc_done, Q + (ADA_FIRST + 1))
                pe.wait_ge(mods_done, Q + ADA_FIRST)
                for c in range(4):
                    m = nc.tensor.matmul(ps[:, 6, c:c + 1], ada_acc[:, c * P:(c + 1) * P], ones[:, 0:1],
                                         start=True, stop=True)
                m.then_inc(ada_summed, 1)

            def norm(k, kind="h"):
                pe.wait_ge(acc_done, OUT_PAIRS * (k + 1) + 1)
                for t in range(TT):
                    m = nc.tensor.matmul(ps[:, 4, t:t + 1], acc[:, t * P:(t + 1) * P], ones[:, 0:1],
                                         start=True, stop=True)
                m.then_inc(stat_done, 1)
                pe.wait_ge(rstd_done, k + 1)
                for t in range(TT):
                    m = nc.tensor.matmul(ps[:, 5, t * P:(t + 1) * P], rstd[:, t:t + 1].broadcast_to([P, P]), ident[:],
                                         start=True, stop=True)
                m.then_inc(rbc_done, 1)
                if kind == "out":
                    for t in range(KT):
                        pe.wait_ge(hf_done, KT * k + t + 1)
                        if t >= 2:
                            pe.wait_ge(y_copied, t - 1)
                        for j in range(TT):
                            m = nc.tensor.transpose(ps[:, t % 2, j * P:(j + 1) * P],
                                                    slots[t % 4][:, j * P:(j + 1) * P], ident[:])
                        m.then_inc(y_turned, 1)

            def out_phase(n0, chunks, pair0, xh, xl, ada=None, g_all=None):
                m = len(chunks)
                with pe.Fori(0, 2) as j:
                    n = j * (2 * m) + n0
                    for dp in range(2):
                        pe.wait_ge(x_done, j * 2 + (pair0 + dp))
                        for c, r in enumerate(chunks):
                            k = dp * m + c
                            if c == m - 1 and g_all is not None:
                                pe.wait_ge(g_lo_done, g_all)
                            chunk(n + k, k, xh, xl, 8 * c, r, 2 * dp, c == 0, c == m - 1)
                        if ada is not None:
                            ada_sum(j * 2 + (ada + dp))

            def ffn(f):
                n0 = C_FFN[f]
                a_in, a_out = ADA_AT[f]
                hk = HK[NORM_OF[f]] * KT
                def in_pair(i, ada):
                    pe.wait_ge(silu_done, i + (FFN_PAIRS * f + 1))
                    chunk(i * 2 + n0, 0, h_hi, h_lo, 0, 8, 0, True, True, h_from=hk)
                    pe.wait_ge(prod_done, i + (FFN_PAIRS * f + 1))
                    chunk(i * 2 + (n0 + 1), 1, h_hi, h_lo, 0, 8, 2, True, True)
                    if ada:
                        ada_sum(i + a_in)
                with pe.Fori(0, ADA_IN) as i:
                    in_pair(i, a_in is not None)
                in_pair(ADA_IN, False)
                pe.wait_ge(silu_done, FFN_PAIRS * (f + 1) + 1)
                pe.wait_ge(g_lo_done, FFN_PAIRS * (f + 1))
                out_phase(n0 + 2 * FFN_PAIRS, FFN_OUT, OUT_PAIRS * (SUB[f] + 1), g_hi, g_lo, a_out,
                          FFN_PAIRS * (f + 1) + 1)

            def retention():
                hk = HK[1] * KT
                with pe.Fori(0, HEADS) as h:
                    n = h * 6 + C_RET
                    chunk(n, 0, h_hi, h_lo, 0, 8, 0, True, True, h_from=hk)
                    pe.wait_ge(o_t_done, h * TT + 1)
                    chunk(n + 1, 1, h_hi, h_lo, 0, 8, 2, True, True)
                    pe.wait_ge(silu_g_done, h * 2 + 1)
                    values(n, 0)
                    pe.wait_ge(rot_lo_done, h * 2 + 3)
                    scores(h, 0)
                    values(n, 1)
                    pe.wait_ge(v_lo_done, h * 2 + 3)
                    weighted(h, 0)
                    scores(h, 1)
                    gate_tile(n, 0)
                    weighted(h, 1)
                    turn(h, 0)
                    scores(h, 2)
                    gate_tile(n, 1)
                    weighted(h, 2)
                    turn(h, 1)
                    scores(h, 3)
                    gate_tile(n, 2)
                    weighted(h, 3)
                    turn(h, 2)
                    gate_tile(n, 3)
                    turn(h, 3)

            def values(n, e):
                pe.wait_ge(w_lo_done, n + (e + 4))
                for t in range(TT):
                    o = ps[:, 4 + 2 * e + t // 2, (t % 2) * CW:(t % 2 + 1) * CW]
                    for r in range(KT):
                        at = slice(t * P, (t + 1) * P)
                        m = mm3(o, h_hi[:, r, at], h_lo[:, r, at], w_hi[e][:, r, :], w_lo[e][:, r, :],
                                r == 0, r == KT - 1)
                m.then_inc(w_used, 1)

            def gate_tile(n, i):
                e, c = i // 2, slice(i % 2 * P, (i % 2 + 1) * P)
                if i % 2 == 0:
                    pe.wait_ge(w_lo_done, n + (e + 6))
                for r in range(KT):
                    m = mm3(ps[:, 4 + i], w_hi[e][:, r, c], w_lo[e][:, r, c], h_hi[:, r], h_lo[:, r], r == 0, r == KT - 1)
                if i % 2:
                    m.then_inc(w_used, 1)

            def weighted(h, I):
                pe.wait_ge(s_lo_done, h * TT + (I + 1))
                for J in range(I + 1):
                    at = slice(J * P, (J + 1) * P)
                    m = mm3(ps[:, 1 + I % 2], s_hi[:, at], s_lo[:, at], v_hi[:, J], v_lo[:, J], J == 0, J == I)
                m.then_inc(pv_done, 1)

            def turn(h, I):
                pe.wait_ge(o_normed, h * TT + (I + 1))
                pe.wait_ge(o_t_done, h * TT + (I + 1))
                for t in range(TT):
                    m = nc.tensor.transpose(ps[:, 3, t * P:(t + 1) * P], o_n[:, t * P:(t + 1) * P], ident[:])
                m.then_inc(o_turned, 1)

            def scores(h, I):
                Q = slice(I * P, (I + 1) * P)
                for J in range(I + 1):
                    K = slice(J * P, (J + 1) * P)
                    for t in range(2):
                        m = mm3(ps[:, 0, K], k_hi[:, t, K], k_lo[:, t, K], q_hi[:, t, Q], q_lo[:, t, Q], t == 0, t == 1)
                m.then_inc(score_done, 1)

            def s5():
                T_ = nc.tensor.transpose
                pe.wait_ge(nat_in, 16 * 10)
                for r in range(2):
                    m = T_(ps[:, 7, r * G:(r + 1) * G], a_nat[:, r], ident[0:NS, 0:NS])
                m.then_inc(nat_turned, 1)
                for r in range(2):
                    bk = b_nat[:, r].rearrange("g (p k) -> g k p", k=SK)
                    for k in range(SK):
                        m = T_(ps[0:NS, 2 * r + k // 8, (k % 8) * G:(k % 8 + 1) * G],
                               bk[:, k, :], ident[0:NS, 0:NS])
                    m.then_inc(nat_turned, 1)
                pe.wait_ge(xn_done, 1 + 5 * KT)
                pe.wait_ge(a_copied, 1)
                for r in range(2):
                    if r:
                        pe.wait_ge(bank7_read, 1)
                    for t in range(KT):
                        m = T_(ps[:, 4 + 2 * r + t // 4, (t % 4) * P:(t % 4 + 1) * P], c_nat[:, r, t], ident[:])
                    m.then_inc(nat_turned, 1)
                pe.wait_ge(nat_copied, 4)
                for s in (y_done, yz_turned):
                    pe.sem_inc(s, 1)

                def front(b, s, first=False):
                    pe.wait_ge(ub_done, b + 1)
                    if not first:
                        pe.wait_ge(yz_done, b)
                    pe.sem_inc(pe_passed, 1)
                    ub = s_buf[:, 1].rearrange("p (c j) -> p j c", j=SC)
                    for j in range(SC):
                        m = T_(ps[0:NC, j // 4, (j % 4) * P:(j % 4 + 1) * P], ub[:, SC - 1 - j, :], ident[:])
                    m.then_inc(u_turned, 1)
                    pe.wait_ge(xs_done, b + 1)
                    if not first:
                        pe.wait_ge(win_done, b)
                    pe.sem_inc(pe_passed, 1)
                    for g in range(GB):
                        m = T_(ps[:, 3 + g // 4, (g % 4) * P:(g % 4 + 1) * P],
                               xs[:, g].rearrange("p j k -> p (j k)"), ident[:])
                    m.then_inc(xs_turned, 1)
                    pe.wait_ge(ys_done, b + 1)
                    pe.wait_ge(rows_done, b + 1)
                    if not first:
                        pe.wait_ge(m_done, b)
                    for g in range(GB):
                        m = nc.tensor.matmul(ps[:, 5 + g // 4, (g % 4) * P:(g % 4 + 1) * P], b_rows[:, g],
                                             ys[:, s, g, 0:SC, :].rearrange("p d k -> p (d k)"),
                                             start=True, stop=True)
                    m.then_inc(lag_done, 1)
                    pe.wait_ge(z_done, b + 1)
                    if not first:
                        pe.wait_ge(yd_done, b)
                    pe.sem_inc(pe_passed, 1)
                    for g in range(GB):
                        m = T_(ps[:, 2, g * NC:(g + 1) * NC], zt[:, g * P:(g + 1) * P], ident[0:NC, 0:NC])
                    m.then_inc(z_turned, 1)

                def states(b, s):
                    pe.wait_ge(win_done, b + 1)
                    pe.wait_ge(us_done, b + 1)
                    if not (isinstance(b, int) and b == 0):
                        pe.wait_ge(sp_done, b)
                    for g in range(GB):
                        m = nc.tensor.matmul(ps[:, 7, g * NC:(g + 1) * NC], win[:, g], us[:, s, g],
                                             start=True, stop=True)
                    m.then_inc(v_done, 1)

                def outputs(b, s):
                    pe.wait_ge(m_done, b + 1)
                    pe.wait_ge(sp_done, b + 1)
                    for g in range(GB):
                        o = ps[0:NC, g // 4, (g % 4) * P:(g % 4 + 1) * P]
                        nc.tensor.matmul(o, us[:, s, g], mt[:, s, g], start=True, stop=False)
                        m = nc.tensor.matmul(o, s_prev[:, g], ys[:, s, g, 1:SC + 1, :].rearrange("p d k -> p (d k)"),
                                             start=False, stop=True)
                    m.then_inc(y_done, 1)

                def turn_back(b):
                    pe.wait_ge(yz_done, b + 2)
                    pe.sem_inc(pe_passed, 1)
                    for i in range(SC):
                        m = T_(ps[:, 2, i * NC:(i + 1) * NC], zt[:, i * P:(i + 1) * P], ident[0:NC, 0:NC])
                    m.then_inc(yz_turned, 1)

                front(0, 0, True)
                states(0, 0)
                with pe.Fori(0, KT // 2 - 1) as i:
                    for s in range(2):
                        front(i * 2 + (s + 1), 1 - s)
                        states(i * 2 + (s + 1), 1 - s)
                        outputs(i * 2 + s, s)
                        turn_back(i * 2 + s)
                front(KT - 1, 1)
                states(KT - 1, 1)
                outputs(KT - 2, 0)
                turn_back(KT - 2)
                outputs(KT - 1, 1)
                turn_back(KT - 1)
                pe.wait_ge(a5_lo, KT + 1)
                pe.wait_ge(m_early, KT)
                with pe.Fori(0, OUT_PAIRS) as dp:
                    n = dp * 2 + C_GLU
                    pe.wait_ge(x_done, dp + (5 * OUT_PAIRS + 1))
                    chunk(n, 0, h_hi, h_lo, 0, 8, 0, True, True)
                    chunk(n + 1, 1, h_hi, h_lo, 0, 8, 2, True, True)

            for s in (w_used, o_turned):
                pe.sem_inc(s, 1)
            pe.wait_ge(consts, 4)
            pe.wait_ge(rows_in, 16 * 7)
            for r in range(3):
                m = nc.tensor.transpose(ps[:, 7, 72 * r:72 * r + 72], sq[0:72, 0, r * P:(r + 1) * P],
                                        ident[0:72, 0:72])
            m.then_inc(rows_turned, 1)
            for t in range(TT):
                pe.wait_ge(x_in[t], 16)
            for k in range(KT):
                if k >= 4 and k % 2 == 0:
                    pe.wait_ge(x_copied, (k - 4) // 2 + 1)
                for t in range(TT):
                    m = nc.tensor.transpose(ps[:, k % 4, t * P:(t + 1) * P], x_tok[:, t, k * P:(k + 1) * P], ident[:])
                m.then_inc(x_turned, 1)
            for q in range(ADA_FIRST):
                pe.wait_ge(ada_acc_done, q + 1)
                if q:
                    pe.wait_ge(mods_done, q)
                for c in range(4):
                    m = nc.tensor.matmul(ps[:, 6, c:c + 1], ada_acc[:, c * P:(c + 1) * P], ones[:, 0:1],
                                         start=True, stop=True)
                m.then_inc(ada_summed, 1)
            norm(0)
            ffn(0)
            norm(1)
            retention()
            pe.wait_ge(a_lo_done, 1 + HEADS * 2)
            out_phase(C_RET_OUT, RET_OUT, OUT_PAIRS * 2, g_hi, g_lo)
            norm(2)
            ffn(1)
            norm(3)
            ffn(2)
            norm(4)
            s5()
            norm(5)
            ffn(3)
            norm(6, "out")


NORM_OF = {0: 0, 1: 2, 2: 3, 3: 5}
SUB = {0: 0, 1: 2, 2: 3, 3: 5}
HK = {0: 0, 1: 1, 2: 2, 3: 3, 5: 4}
MODS_NEED = {0: 4, 1: 18, 2: 18, 3: 32, 4: 36, 5: 36}


def landed(n, k):
    return (n - k % 2) * 8 + 16


_INS = ["x", "c", "positions", "ada_w", "ada_b", "norm_g", "ffn_w_in", "ffn_w_out", "ret_w_in", "ret_w_out",
        "s5_a_re", "s5_a_im", "s5_b_re", "s5_b_im", "s5_c_re", "s5_c_im", "s5_d", "s5_log_dt", "s5_w_glu", "final_g"]


def shape_constants():
    half = D // HEADS // 2
    inv_freq = (np.float32(10000.0) ** (-np.arange(half, dtype=np.float32) / np.float32(half))).astype(np.float32)
    log_gamma = np.log(1.0 - 2.0 ** (-5.0 - np.arange(HEADS)))
    c, j = np.arange(L)[None, None, :], np.arange(P)[None, :, None]
    decay = np.where(c >= j, np.exp(log_gamma[:, None, None] * np.maximum(c - j, 0)), 0.0)
    p = np.arange(P)
    s5_const = np.concatenate([np.where(p < NS, 1.0, -1.0)[:, None], (p // SK % 2 == 0)[:, None],
                               (p // SK % 2 == 1)[:, None], np.repeat(np.arange(NC)[None] > 0, P, 0)], 1)
    return {"s5_const": s5_const.astype(np.float32), "inv_freq": inv_freq[:, None],
            "decay": (decay / np.sqrt(D // HEADS)).astype(np.float32)}


def kernel(**inputs):
    import numpy as _np
    import concourse.bacc as _bacc
    from concourse.bass_utils import run_bass_kernel_spmd as _run

    nc = _bacc.Bacc("TRN2", target_bir_lowering=False, num_devices=1)
    arrays, ins = {}, {}
    for name, a in [(n, inputs[n]) for n in _INS] + list(shape_constants().items()):
        a = _np.ascontiguousarray(a)
        arrays[f"in_{name}"] = a
        ins[name] = nc.dram_tensor(f"in_{name}", a.shape, mybir.dt.from_np(a.dtype), kind="ExternalInput").ap()
    out = nc.dram_tensor("out_y", (1, L, D), F32, kind="ExternalOutput").ap()
    build(nc, ins, out)
    r = _run(nc, [arrays], core_ids=[0])
    return r.results[0]["out_y"]
```
